# Optimizing a Trainium2 kernel written in Bass

```python
import jax, jax.numpy as jnp
from jax import lax
import numpy as np
import math

D_MODEL = 1024
BATCH = 1
SEQ = 256
DEPTH = 2

CHUNK = 64
Q_BLOCK = 128
PLE_DIM = 256

MLA_HEADS = 16
MLA_Q_LORA = D_MODEL // 2
MLA_KV_LORA = D_MODEL // 4
MLA_NOPE = 128
MLA_ROPE = 64
MLA_V = 128
ROPE_THETA = 10000.0

GLA_HEADS = 4
GLA_QK = D_MODEL // 2
GLA_VD = D_MODEL
GLA_DK = GLA_QK // GLA_HEADS
GLA_DV = GLA_VD // GLA_HEADS
GLA_GATE_RANK = 16
GLA_TAU = 16.0

D_FF = 2816
CONV_W = 3

N_MLA = (DEPTH + 1) // 2
N_GLA = DEPTH // 2
DN_ALPHA = (2 * DEPTH) ** 0.25
DN_BETA = (8 * DEPTH) ** -0.25
EPS = 1e-5
NEG_INF = -1e30


def layer_norm(x, g, b):
    xf = x.astype(jnp.float32)
    mu = jnp.mean(xf, -1, keepdims=True)
    var = jnp.mean(jnp.square(xf - mu), -1, keepdims=True)
    return ((xf - mu) * lax.rsqrt(var + EPS) * g + b).astype(x.dtype)

def rms_norm(x, g):
    xf = x.astype(jnp.float32)
    return (xf * lax.rsqrt(jnp.mean(jnp.square(xf), -1, keepdims=True) + EPS) * g).astype(x.dtype)

def rope_tables(positions):
    inv = 1.0 / (ROPE_THETA ** (jnp.arange(0, MLA_ROPE, 2, dtype=jnp.float32) / MLA_ROPE))
    ang = positions.astype(jnp.float32)[..., None] * inv
    return jnp.cos(ang), jnp.sin(ang)

def apply_rope(x, cos, sin):
    x1, x2 = jnp.split(x, 2, axis=-1)
    c = cos.astype(x.dtype)
    s = sin.astype(x.dtype)
    return jnp.concatenate([x1 * c - x2 * s, x1 * s + x2 * c], axis=-1)

def mla_mixer(x, positions, cos, sin, w_in, q_norm, kv_norm, w_uq, w_uk, w_uv, w_o):
    B, S, _ = x.shape
    h = x @ w_in
    c_q, c_kv, k_r = jnp.split(h, [MLA_Q_LORA, MLA_Q_LORA + MLA_KV_LORA], axis=-1)
    c_q = rms_norm(c_q, q_norm)
    c_kv = rms_norm(c_kv, kv_norm)
    q = (c_q @ w_uq).reshape(B, S, MLA_HEADS, MLA_NOPE + MLA_ROPE)
    q_nope = q[..., :MLA_NOPE]
    q_rope = apply_rope(q[..., MLA_NOPE:], cos[:, :, None], sin[:, :, None])
    k_rope = apply_rope(k_r, cos, sin)
    k_nope = (c_kv @ w_uk).reshape(B, S, MLA_HEADS, MLA_NOPE)
    v = (c_kv @ w_uv).reshape(B, S, MLA_HEADS, MLA_V)
    scale = (MLA_NOPE + MLA_ROPE) ** -0.5
    chunk_id = positions // CHUNK
    outs = []
    for blk in range(S // Q_BLOCK):
        q0 = blk * Q_BLOCK
        q1 = q0 + Q_BLOCK
        s = (jnp.einsum('bqhd,bkhd->bhqk', q_nope[:, q0:q1], k_nope[:, :q1])
             + jnp.einsum('bqhr,bkr->bhqk', q_rope[:, q0:q1], k_rope[:, :q1])).astype(jnp.float32) * scale
        mask = chunk_id[:, None, :q1] <= chunk_id[:, q0:q1, None]
        s = jnp.where(mask[:, None], s, NEG_INF)
        pr = jax.nn.softmax(s, axis=-1).astype(v.dtype)
        outs.append(jnp.einsum('bhqk,bkhd->bqhd', pr, v[:, :q1]))
    o = jnp.concatenate(outs, axis=1).reshape(B, S, MLA_HEADS * MLA_V)
    return (o @ w_o).astype(x.dtype)

def gla_mixer(x, w_in, w_a2, b_a, o_norm, w_o):
    B, S, _ = x.shape
    N = S // CHUNK
    h = x @ w_in
    q, k, v, r, a = jnp.split(h, [GLA_QK, 2 * GLA_QK, 2 * GLA_QK + GLA_VD, 2 * GLA_QK + 2 * GLA_VD], axis=-1)
    log_a = jax.nn.log_sigmoid((a @ w_a2 + b_a).astype(jnp.float32)) / GLA_TAU
    q = q.reshape(B, N, CHUNK, GLA_HEADS, GLA_DK) * (GLA_DK ** -0.5)
    k = k.reshape(B, N, CHUNK, GLA_HEADS, GLA_DK)
    v = v.reshape(B, N, CHUNK, GLA_HEADS, GLA_DV)
    log_a = log_a.reshape(B, N, CHUNK, GLA_HEADS, GLA_DK)
    cum = jnp.cumsum(log_a, axis=2)
    tot = cum[:, :, -1]
    k_dec = k * jnp.exp(tot[:, :, None] - cum).astype(k.dtype)
    upd = jnp.einsum('bnchk,bnchv->nbhkv', k_dec, v).astype(jnp.float32)
    decay = jnp.exp(jnp.moveaxis(tot, 1, 0))
    q_n = jnp.moveaxis(q, 1, 0)

    def step(state, inp):
        g, u, qc = inp
        state = state * g[..., None] + u
        return state, jnp.einsum('bchk,bhkv->bchv', qc, state)

    state0 = jnp.zeros((B, GLA_HEADS, GLA_DK, GLA_DV), jnp.float32)
    _, o = lax.scan(step, state0, (decay, upd, q_n))
    o = jnp.moveaxis(o, 0, 1).reshape(B, S, GLA_HEADS, GLA_DV)
    mu = jnp.mean(o, -1, keepdims=True)
    var = jnp.mean(jnp.square(o - mu), -1, keepdims=True)
    o = (o - mu) * lax.rsqrt(var + EPS) * o_norm.reshape(GLA_HEADS, GLA_DV)
    o = o.reshape(B, S, GLA_VD).astype(x.dtype) * jax.nn.silu(r)
    return (o @ w_o).astype(x.dtype)

def conv_ffn(x, w_up, conv_w, conv_b, w_down):
    S = x.shape[1]
    h = x @ w_up
    hp = jnp.pad(h, ((0, 0), (CONV_W - 1, 0), (0, 0)))
    h = hp[:, 0:S] * conv_w[0] + hp[:, 1:S + 1] * conv_w[1] + hp[:, 2:S + 2] * conv_w[2] + conv_b
    u, g = jnp.split(h, 2, axis=-1)
    return ((u * jax.nn.gelu(g)) @ w_down).astype(x.dtype)

def first_inputs(seed: int = 0) -> dict:
    key = jax.random.key(seed)
    ks = iter(jax.random.split(key, 40))
    f32 = jnp.float32

    def nrm(shape, scale):
        return jax.random.normal(next(ks), shape, f32) * scale

    def gain(shape):
        return 1.0 + nrm(shape, 0.01)

    x = jax.random.normal(next(ks), (BATCH, SEQ, D_MODEL), f32)
    p = jax.random.normal(next(ks), (DEPTH, BATCH, SEQ, PLE_DIM), f32)
    offsets = jax.random.randint(next(ks), (BATCH, 1), 0, 16, dtype=jnp.int32) * CHUNK
    positions = (jnp.arange(SEQ, dtype=jnp.int32)[None, :] + offsets).astype(jnp.int32)

    mla_in = MLA_Q_LORA + MLA_KV_LORA + MLA_ROPE
    gla_in = 2 * GLA_QK + 2 * GLA_VD + GLA_GATE_RANK
    return {
        "x": x,
        "p": p,
        "positions": positions,
        "mla_w_in": nrm((N_MLA, D_MODEL, mla_in), D_MODEL ** -0.5),
        "mla_q_norm": gain((N_MLA, MLA_Q_LORA)),
        "mla_kv_norm": gain((N_MLA, MLA_KV_LORA)),
        "mla_w_uq": nrm((N_MLA, MLA_Q_LORA, MLA_HEADS * (MLA_NOPE + MLA_ROPE)), MLA_Q_LORA ** -0.5),
        "mla_w_uk": nrm((N_MLA, MLA_KV_LORA, MLA_HEADS * MLA_NOPE), MLA_KV_LORA ** -0.5),
        "mla_w_uv": nrm((N_MLA, MLA_KV_LORA, MLA_HEADS * MLA_V), DN_BETA * MLA_KV_LORA ** -0.5),
        "mla_w_o": nrm((N_MLA, MLA_HEADS * MLA_V, D_MODEL), DN_BETA * (MLA_HEADS * MLA_V) ** -0.5),
        "gla_w_in": nrm((N_GLA, D_MODEL, gla_in), D_MODEL ** -0.5),
        "gla_w_a2": nrm((N_GLA, GLA_GATE_RANK, GLA_QK), GLA_GATE_RANK ** -0.5),
        "gla_b_a": nrm((N_GLA, GLA_QK), 0.1),
        "gla_o_norm": gain((N_GLA, GLA_VD)),
        "gla_w_o": nrm((N_GLA, GLA_VD, D_MODEL), DN_BETA * GLA_VD ** -0.5),
        "ln1_g": gain((DEPTH, D_MODEL)),
        "ln1_b": nrm((DEPTH, D_MODEL), 0.01),
        "ln2_g": gain((DEPTH, D_MODEL)),
        "ln2_b": nrm((DEPTH, D_MODEL), 0.01),
        "ffn_w_up": nrm((DEPTH, D_MODEL, 2 * D_FF), D_MODEL ** -0.5),
        "ffn_conv_w": nrm((DEPTH, CONV_W, 2 * D_FF), CONV_W ** -0.5),
        "ffn_conv_b": nrm((DEPTH, 2 * D_FF), 0.01),
        "ffn_w_down": nrm((DEPTH, D_FF, D_MODEL), DN_BETA * D_FF ** -0.5),
        "ple_w_proj": nrm((DEPTH, PLE_DIM, D_MODEL), PLE_DIM ** -0.5),
        "ple_w_gate": nrm((DEPTH, D_MODEL, D_MODEL), D_MODEL ** -0.5),
        "ple_b_gate": nrm((DEPTH, D_MODEL), 0.01),
    }

def first_block(x, p, positions, mla_w_in, mla_q_norm, mla_kv_norm, mla_w_uq, mla_w_uk, mla_w_uv, mla_w_o,
              gla_w_in, gla_w_a2, gla_b_a, gla_o_norm, gla_w_o, ln1_g, ln1_b, ln2_g, ln2_b,
              ffn_w_up, ffn_conv_w, ffn_conv_b, ffn_w_down, ple_w_proj, ple_w_gate, ple_b_gate):
    cos, sin = rope_tables(positions)
    for i in range(DEPTH):
        j = i // 2
        if i % 2 == 0:
            m = mla_mixer(x, positions, cos, sin, mla_w_in[j], mla_q_norm[j], mla_kv_norm[j],
                          mla_w_uq[j], mla_w_uk[j], mla_w_uv[j], mla_w_o[j])
        else:
            m = gla_mixer(x, gla_w_in[j], gla_w_a2[j], gla_b_a[j], gla_o_norm[j], gla_w_o[j])
        x = layer_norm(DN_ALPHA * x + m, ln1_g[i], ln1_b[i])
        x = layer_norm(DN_ALPHA * x + conv_ffn(x, ffn_w_up[i], ffn_conv_w[i], ffn_conv_b[i], ffn_w_down[i]),
                       ln2_g[i], ln2_b[i])
        gate = jax.nn.sigmoid(x @ ple_w_gate[i] + ple_b_gate[i])
        x = x + gate * (p[i] @ ple_w_proj[i])
    return x


N_META = 16
N_A = DEPTH // 2
N_B = DEPTH - N_A
N_HEADS = 8
HEAD_DIM = D_MODEL // N_HEADS
CONV_WIDTH = 3
BLOCK = 128
PAD = (-N_META) % BLOCK
LN_EPS = 1e-5
DEEPNORM_ALPHA = (2 * DEPTH) ** 0.25
DEEPNORM_BETA = (8 * DEPTH) ** -0.25
NEG_INF_2 = -1e30


def layer_norm_2(x, g, b):
    xf = x.astype(jnp.float32)
    mu = jnp.mean(xf, axis=-1, keepdims=True)
    var = jnp.mean(jnp.square(xf - mu), axis=-1, keepdims=True)
    y = (xf - mu) * lax.rsqrt(var + LN_EPS) * g.astype(jnp.float32) + b.astype(jnp.float32)
    return y.astype(x.dtype)

def swiglu(x, wg, wu, wd):
    return (jax.nn.silu(x @ wg) * (x @ wu)) @ wd

def short_conv(x, w_in, w_conv, w_out):
    bgate, cgate, val = jnp.split(x @ w_in, 3, axis=-1)
    u = cgate * val
    y = lax.conv_general_dilated(
        u, w_conv[:, None, :].astype(u.dtype),
        window_strides=(1,), padding=[(CONV_WIDTH - 1, 0)],
        dimension_numbers=("NWC", "WIO", "NWC"),
        feature_group_count=D_MODEL)
    return (bgate * y) @ w_out

def shared_kv(h, kv_w, f_bias):
    bsz, L, _ = h.shape
    kvf = h @ kv_w
    k = kvf[..., :D_MODEL].reshape(bsz, L, N_HEADS, HEAD_DIM)
    v = kvf[..., D_MODEL:2 * D_MODEL].reshape(bsz, L, N_HEADS, HEAD_DIM)
    f_logit = (kvf[..., 2 * D_MODEL:] + f_bias).astype(jnp.float32)
    log_f = jax.nn.log_sigmoid(f_logit)
    pad4 = ((0, 0), (PAD, 0), (0, 0), (0, 0))
    k = jnp.pad(k, pad4).transpose(0, 2, 1, 3)
    v = jnp.pad(v, pad4).transpose(0, 2, 1, 3)
    log_f = jnp.pad(log_f, ((0, 0), (PAD, 0), (0, 0)))
    c = jnp.cumsum(log_f, axis=1).transpose(0, 2, 1)
    return k, v, c

def forgetting_attention(h, w_q, w_o, k, v, c):
    bsz, L, _ = h.shape
    Lp = L + PAD
    n_blocks = Lp // BLOCK
    scale = 1.0 / math.sqrt(HEAD_DIM)
    q = (h @ w_q).reshape(bsz, L, N_HEADS, HEAD_DIM)
    q = jnp.pad(q, ((0, 0), (PAD, 0), (0, 0), (0, 0))).transpose(0, 2, 1, 3)
    k_pos = jnp.arange(Lp)

    def one_block(i):
        start = i * BLOCK
        qb = lax.dynamic_slice_in_dim(q, start, BLOCK, axis=2)
        cq = lax.dynamic_slice_in_dim(c, start, BLOCK, axis=2)
        s = jnp.einsum("bhqd,bhkd->bhqk", qb, k).astype(jnp.float32) * scale
        s = s + cq[..., :, None] - c[..., None, :]
        q_pos = start + jnp.arange(BLOCK)
        mask = (k_pos[None, :] <= q_pos[:, None]) & (k_pos[None, :] >= PAD)
        s = jnp.where(mask, s, NEG_INF_2)
        p = jax.nn.softmax(s, axis=-1)
        return jnp.einsum("bhqk,bhkd->bhqd", p.astype(v.dtype), v)

    o = lax.map(one_block, jnp.arange(n_blocks))
    o = o.transpose(1, 0, 3, 2, 4).reshape(bsz, Lp, D_MODEL)[:, PAD:]
    return o @ w_o

def second_inputs(seed: int = 0) -> dict:
    key = jax.random.key(seed)
    ks = jax.random.split(key, 20)
    f32 = jnp.float32

    def nrm(k, shape, scale):
        return jax.random.normal(k, shape, f32) * scale

    d_s = D_MODEL ** -0.5
    f_s = D_FF ** -0.5
    x = nrm(ks[0], (BATCH, SEQ, D_MODEL), 1.0)
    meta = nrm(ks[1], (N_META, D_MODEL), 1.0)
    ffn1_wg = nrm(ks[2], (DEPTH, D_MODEL, D_FF), d_s)
    ffn1_wu = nrm(ks[3], (DEPTH, D_MODEL, D_FF), d_s)
    ffn1_wd = nrm(ks[4], (DEPTH, D_FF, D_MODEL), f_s * DEEPNORM_BETA)
    ffn2_wg = nrm(ks[5], (DEPTH, D_MODEL, D_FF), d_s)
    ffn2_wu = nrm(ks[6], (DEPTH, D_MODEL, D_FF), d_s)
    ffn2_wd = nrm(ks[7], (DEPTH, D_FF, D_MODEL), f_s * DEEPNORM_BETA)
    ln_gain = 1.0 + nrm(ks[8], (DEPTH, 3, D_MODEL), 0.02)
    ln_bias = nrm(ks[9], (DEPTH, 3, D_MODEL), 0.02)
    conv_w_in = nrm(ks[10], (N_A, D_MODEL, 3 * D_MODEL), d_s)
    conv_w = nrm(ks[11], (N_A, CONV_WIDTH, D_MODEL), CONV_WIDTH ** -0.5)
    conv_w_out = nrm(ks[12], (N_A, D_MODEL, D_MODEL), d_s * DEEPNORM_BETA)
    w_k = nrm(ks[13], (D_MODEL, D_MODEL), d_s)
    w_v = nrm(ks[14], (D_MODEL, D_MODEL), d_s * DEEPNORM_BETA)
    w_f = nrm(ks[15], (D_MODEL, N_HEADS), d_s * 0.5)
    kv_w = jnp.concatenate([w_k, w_v, w_f], axis=1)
    f_bias = 3.0 + nrm(ks[16], (N_HEADS,), 0.5)
    attn_w_q = nrm(ks[17], (N_B, D_MODEL, D_MODEL), d_s)
    attn_w_o = nrm(ks[18], (N_B, D_MODEL, D_MODEL), d_s * DEEPNORM_BETA)
    return {"x": x, "meta": meta,
            "ffn1_wg": ffn1_wg, "ffn1_wu": ffn1_wu, "ffn1_wd": ffn1_wd,
            "ffn2_wg": ffn2_wg, "ffn2_wu": ffn2_wu, "ffn2_wd": ffn2_wd,
            "ln_gain": ln_gain, "ln_bias": ln_bias,
            "conv_w_in": conv_w_in, "conv_w": conv_w, "conv_w_out": conv_w_out,
            "kv_w": kv_w, "f_bias": f_bias,
            "attn_w_q": attn_w_q, "attn_w_o": attn_w_o}

def second_block(x, meta, ffn1_wg, ffn1_wu, ffn1_wd, ffn2_wg, ffn2_wu, ffn2_wd,
              ln_gain, ln_bias, conv_w_in, conv_w, conv_w_out, kv_w, f_bias,
              attn_w_q, attn_w_o):
    bsz = x.shape[0]
    h = jnp.concatenate(
        [jnp.broadcast_to(meta.astype(x.dtype)[None], (bsz, N_META, D_MODEL)), x], axis=1)
    k_sh = v_sh = c_sh = None
    for l in range(DEPTH):
        h = layer_norm_2(DEEPNORM_ALPHA * h + 0.5 * swiglu(h, ffn1_wg[l], ffn1_wu[l], ffn1_wd[l]),
                       ln_gain[l, 0], ln_bias[l, 0])
        if l < N_A:
            mix = short_conv(h, conv_w_in[l], conv_w[l], conv_w_out[l])
        else:
            j = l - N_A
            mix = forgetting_attention(h, attn_w_q[j], attn_w_o[j], k_sh, v_sh, c_sh)
        h = layer_norm_2(DEEPNORM_ALPHA * h + mix, ln_gain[l, 1], ln_bias[l, 1])
        h = layer_norm_2(DEEPNORM_ALPHA * h + 0.5 * swiglu(h, ffn2_wg[l], ffn2_wu[l], ffn2_wd[l]),
                       ln_gain[l, 2], ln_bias[l, 2])
        if l == N_A - 1:
            k_sh, v_sh, c_sh = shared_kv(h, kv_w, f_bias)
    return h[:, N_META:]


def setup_inputs(seed=0):
    out = dict(first_inputs(seed))
    for name, value in second_inputs(seed + 1).items():
        if name != "x":
            out[name + "_2"] = value
    return out


def reference(
    x, p, positions, mla_w_in, mla_q_norm, mla_kv_norm, mla_w_uq, mla_w_uk, mla_w_uv, mla_w_o,
    gla_w_in, gla_w_a2, gla_b_a, gla_o_norm, gla_w_o, ln1_g, ln1_b, ln2_g, ln2_b, ffn_w_up,
    ffn_conv_w, ffn_conv_b, ffn_w_down, ple_w_proj, ple_w_gate, ple_b_gate, meta_2, ffn1_wg_2,
    ffn1_wu_2, ffn1_wd_2, ffn2_wg_2, ffn2_wu_2, ffn2_wd_2, ln_gain_2, ln_bias_2, conv_w_in_2,
    conv_w_2, conv_w_out_2, kv_w_2, f_bias_2, attn_w_q_2, attn_w_o_2,
):
    x = first_block(
        x, p, positions, mla_w_in, mla_q_norm, mla_kv_norm, mla_w_uq, mla_w_uk, mla_w_uv,
        mla_w_o, gla_w_in, gla_w_a2, gla_b_a, gla_o_norm, gla_w_o, ln1_g, ln1_b, ln2_g, ln2_b,
        ffn_w_up, ffn_conv_w, ffn_conv_b, ffn_w_down, ple_w_proj, ple_w_gate, ple_b_gate,
    )
    return second_block(
        x, meta_2, ffn1_wg_2, ffn1_wu_2, ffn1_wd_2, ffn2_wg_2, ffn2_wu_2, ffn2_wd_2, ln_gain_2,
        ln_bias_2, conv_w_in_2, conv_w_2, conv_w_out_2, kv_w_2, f_bias_2, attn_w_q_2,
        attn_w_o_2,
    )


_drawn_inputs = setup_inputs


def setup_inputs(seed=0):
    import zlib

    import numpy as np

    out = dict(_drawn_inputs(seed))
    spreads = {}
    factors = {'mla_q_norm': 8.0,
     'mla_kv_norm': 8.0,
     'mla_w_uk': 2.784,
     'gla_b_a': 5.992,
     'gla_o_norm': 33.534,
     'ln1_g': 3.667,
     'ln1_b': 3.928,
     'ln2_g': 3.893,
     'ln2_b': 3.982,
     'ffn_conv_b': 8.0,
     'ple_b_gate': 54.844,
     'f_bias_2': 60.552}
    for name, (base, spread) in spreads.items():
        noise = np.random.default_rng([zlib.crc32(name.encode()), seed]).standard_normal(out[name].shape)
        drawn = base * np.exp(spread * noise) if base else spread * noise
        out[name] = __import__('jax').numpy.asarray(drawn.astype(out[name].dtype))
    for name, factor in factors.items():
        out[name] = (out[name] * factor).astype(out[name].dtype)
    return out
```

```python
from contextlib import ExitStack

import numpy as np

import concourse.bass as bass
from concourse import mybir

F32 = mybir.dt.float32
F32R = mybir.dt.float32r
I32 = mybir.dt.int32
ALU = mybir.AluOpType
ACT = mybir.ActivationFunctionType
AX_X = mybir.AxisListType.X

P = 128
D = 1024
KD = D // P
SEQ = 256
META = 16
T = META + SEQ
TOK = slice(META, T)
FF = 2816
NF = FF // P
UNIT = 8 * P
RING = 4
CHUNK = 64
ALPHA = 4 ** 0.25
EPS = 1e-5
NEG = -1e30
MLA_SCALE = 192 ** -0.5
ATT_SCALE = 128 ** -0.5
GLA_SCALE = 128 ** -0.5
GLA_TAU = 16.0
TWO_PI = 2 * np.pi
MAGIC = 1.5 * 2 ** 23

PHASES = [("mla_in", 7)]
for _half in (0, 1):
    PHASES += [(f"mla_qn{_half}", 4), (f"mla_qr{_half}", 2), (f"mla_kn{_half}", 2), (f"mla_v{_half}", 2)]
PHASES += [("mla_o", 16), ("up0", 44), ("down0", 22), ("proj0", 2), ("gate0", 8),
           ("gla_a", 1), ("gla_k", 4), ("gla_v", 8), ("gla_q", 4), ("gla_r", 8), ("gla_o", 8),
           ("up1", 44), ("down1", 22), ("proj1", 2), ("gate1", 8),
           ("up2", 44), ("down2", 22), ("conv_in", 24), ("conv_out", 8), ("up3", 44), ("down3", 22),
           ("kv_k", 8), ("kv_v", 8), ("kv_f", 1),
           ("up4", 44), ("down4", 22), ("att_q", 8), ("att_o", 8), ("up5", 44), ("down5", 22)]
BASE = {}
UNITS = 0
for _name, _n in PHASES:
    BASE[_name] = UNITS
    UNITS += _n

LN = {"mla": 0, "ffn0": 1, "gla": 2, "ffn1": 3, "ffn2": 4, "conv": 5, "ffn3": 6, "ffn4": 7, "att": 8, "ffn5": 9}
X_SPLIT = {}
for _i, _s in enumerate(["init", "ln0", "ln1", "ple0", "ln2", "ln3", "ple1", "ln4", "ln5", "ln6", "ln7", "ln8"]):
    X_SPLIT[_s] = 8 * _i
H_SPLIT = {}
_c = 0
for _s, _n in (("mla", 16), ("ffn0", NF), ("gla", 8), ("ffn1", NF), ("ffn2", NF), ("conv", 8),
               ("ffn3", NF), ("ffn4", NF), ("att", 8), ("ffn5", NF)):
    H_SPLIT[_s] = _c
    _c += _n
CONV_FFNS = (0, 1)

VECS = [("q_norm", 4), ("kv_norm", 2), ("o_norm", 8), ("ln_g", 10 * 8), ("ln_b", 10 * 8),
        ("conv_w", 2 * 3 * 2 * NF), ("conv_b", 2 * 2 * NF), ("ple_b", 2 * 8), ("sconv_w", 3 * 8), ("f_bias", 1)]
COL = {}
NPAR = 0
for _name, _n in VECS:
    COL[_name] = NPAR
    NPAR += _n
CONSTS = [("ident", P), ("suffix", P), ("swap", P), ("chunk_of", 2), ("inv_freq", 1), ("rope_sign", 1), ("one16", 1)]
CCOL = {}
NCON = 0
for _name, _n in CONSTS:
    CCOL[_name] = NCON
    NCON += _n


def ffn_cols(f):
    return slice(0, T) if f in (2, 3) else TOK


def build(nc, stream, xT, metaT, pT, pos, params, consts, causal, wa2, out):
    ctx = ExitStack()
    with ctx:
        def sb(name, shape, dt=F32):
            return ctx.enter_context(nc.sbuf_tensor(name, shape, dt))

        def sem(name):
            return ctx.enter_context(nc.semaphore(name))

        raw = sb("raw", [P, RING, UNIT])
        w_hi = sb("w_hi", [P, RING, UNIT], F32R)
        w_lo = sb("w_lo", [P, RING, UNIT], F32R)
        x = sb("x", [P, KD, T])
        y = sb("y", [P, KD, T])
        a_hi = sb("a_hi", [P, KD, T], F32R)
        a_lo = sb("a_lo", [P, KD, T], F32R)
        b_hi = sb("b_hi", [P, KD, T], F32R)
        b_lo = sb("b_lo", [P, KD, T], F32R)
        h_hi = sb("h_hi", [P, NF, T], F32R)
        h_lo = sb("h_lo", [P, NF, T], F32R)
        work = sb("work", [P, 8192])
        tmp = sb("tmp", [P, 3072])
        mu = sb("mu", [P, T])
        var = sb("var", [P, T])
        acc1 = sb("acc1", [P, T])
        acc2 = sb("acc2", [P, T])
        par = sb("par", [P, NPAR])
        con = sb("con", [P, NCON])
        ones = sb("ones", [P, P])
        cols = sb("cols", [P, 64])
        icol = sb("icol", [P, 4], I32)
        ps = ctx.enter_context(nc.psum_tensor("ps", [P, 8, 512], F32))
        yf = y[:, :, :].rearrange("p k t -> p (k t)")

        def view(buf, at, *dims):
            n = int(np.prod(dims))
            v = buf[:, at:at + n]
            if len(dims) == 2:
                v = v.rearrange("p (a b) -> p a b", a=dims[0])
            return v

        ident = con[:, CCOL["ident"]:CCOL["ident"] + P]
        suffix = con[:, CCOL["suffix"]:CCOL["suffix"] + P]
        swap = con[:, CCOL["swap"]:CCOL["swap"] + P]
        chunk_of = con[:, CCOL["chunk_of"]:CCOL["chunk_of"] + 2]

        def pcol(name, i=0):
            return par[:, COL[name] + i:COL[name] + i + 1]

        def ccol(name):
            return con[:, CCOL[name]:CCOL[name] + 1]

        sq = view(work, 6016, KD, T)
        qn = view(work, 0, 8, SEQ)
        kn = view(work, 2048, 8, SEQ)
        vm = view(work, 4096, 2, 1024)
        qr = view(work, 6144, 4, SEQ)
        c_sq = view(work, 0, 6, SEQ)
        p_raw = view(work, 0, 2, SEQ)
        pp = view(work, 512, 8, SEQ)
        g_q = view(work, 0, 4, SEQ)
        g_rs = view(work, 1024, 8, SEQ)
        g_k = view(work, 3072, 2, 512)
        g_v = view(work, 4096, 2, 1024)
        g_la = view(work, 6144, 2, 512)
        g_wa2 = view(work, 7168, 512)
        g_osq = view(work, 4096, 8, SEQ)
        g_mu = view(work, 3072, 4, SEQ)
        g_var = view(work, 6144, 4, SEQ)
        k_sh = view(work, 0, 8, T)
        v_sh = view(work, 2176, 3, 1024)
        neg_c = view(work, 5248, T)
        cum_c = view(work, 5520, T)
        c_raw = view(yf, 0, 6, SEQ)
        kr_raw = view(yf, 1536, SEQ)
        qr_raw = view(yf, 0, 4, SEQ)
        qr_t = view(yf, 1024, 4, SEQ)
        rope_w = view(yf, 0, 8, SEQ)
        g_t = view(yf, 0, 2, 512)
        g_ed = view(yf, 1024, 2, 512)
        g_o = view(yf, 0, 8, SEQ)
        a_q = view(yf, 0, 8, SEQ)
        f_z = view(yf, 0, T)
        f_t = view(yf, T, T)
        f_one = view(yf, 2 * T, T)
        c_rstd = view(tmp, 1408, 2, SEQ)
        rope_a = view(tmp, 1920, SEQ)
        rope_b = view(tmp, 2176, SEQ)
        cosT = view(tmp, 0, SEQ)
        sinT = view(tmp, 256, SEQ)
        krm = view(tmp, 512, 2, SEQ)
        mask_m = view(tmp, 1024, 384)
        posf = view(tmp, 1408, SEQ)
        posi = view(tmp, 1664, SEQ).bitcast(I32)
        sm_m = view(tmp, 1408, 2, 384)
        pt_m = view(tmp, 2176, 384)
        f_tg = view(tmp, 0, 2, T)
        f_tu = view(tmp, 544, 2, T)
        f_act = view(tmp, 1088, 2, T)
        f_h = view(tmp, 1632, 2, T)
        g_aT = view(tmp, 0, SEQ)
        g_S = view(tmp, 256, 4, 256)
        g_dec = view(tmp, 1280, 4, 4)
        g_h = view(tmp, 1296, 2, SEQ)
        vT = view(tmp, 0, 2, T)
        mask_a = view(tmp, 544, 416)
        sm_a = view(tmp, 960, 2, 416)
        pt_a = view(tmp, 1792, 384)
        ptm_a = view(tmp, 2176, SEQ)
        cq_col = view(tmp, 2432, 2, 8)

        w_landed = [sem(f"w_landed{i}") for i in range(RING)]
        w_hi_ready = sem("w_hi_ready")
        w_lo_ready = sem("w_lo_ready")
        unit_done = sem("unit_done")
        in_x, in_meta, in_pos, in_par, in_con, in_p, in_causal, in_wa2, out_done = (
            sem(n) for n in ("in_x", "in_meta", "in_pos", "in_par", "in_con", "in_p", "in_causal", "in_wa2", "out_done"))
        zeroed = sem("zeroed")
        x_hi_ready = sem("x_hi_ready")
        x_split = sem("x_split")
        meta_split = sem("meta_split")
        h_hi_ready = sem("h_hi_ready")
        h_split = sem("h_split")
        act_step = sem("act_step")
        dve_step = sem("dve_step")
        pool_step = sem("pool_step")
        y_ready = sem("y_ready")
        sq_ready = sem("sq_ready")
        sums_ready = sem("sums_ready")
        stats_ready = sem("stats_ready")
        mean_ready = sem("mean_ready")
        var_ready = sem("var_ready")
        std_ready = sem("std_ready")
        normed = sem("normed")
        x_ready = sem("x_ready")
        rope_arg = sem("rope_arg")
        rope_tab = sem("rope_tab")
        mla_mask = sem("mla_mask")
        c_copied = sem("c_copied")
        c_sums = sem("c_sums")
        c_var = sem("c_var")
        c_std = sem("c_std")
        c_normed = sem("c_normed")
        c_hi = sem("c_hi")
        c_split = sem("c_split")
        kr_swapped = sem("kr_swapped")
        kr_ready = sem("kr_ready")
        q_copied = sem("q_copied")
        qr_copied = sem("qr_copied")
        qr_swapped = sem("qr_swapped")
        qr_ready = sem("qr_ready")
        k_copied = sem("k_copied")
        v_copied = sem("v_copied")
        scores = sem("scores")
        maxed = sem("maxed")
        exped = sem("exped")
        probs = sem("probs")
        turned = sem("turned")
        turned_sb = sem("turned_sb")
        mixed = sem("mixed")
        gate_tap = sem("gate_tap")
        gate_conv = sem("gate_conv")
        gated = sem("gated")
        up_tap = sem("up_tap")
        h_ready = sem("h_ready")
        p_hi = sem("p_hi")
        p_split = sem("p_split")
        pp_copied = sem("pp_copied")
        sig_ready = sem("sig_ready")
        px_ready = sem("px_ready")
        aT_ready = sem("aT_ready")
        z_ready = sem("z_ready")
        ln_ready = sem("ln_ready")
        la_ready = sem("la_ready")
        suf_ready = sem("suf_ready")
        tot_ready = sem("tot_ready")
        ed_ready = sem("ed_ready")
        dec_ready = sem("dec_ready")
        gk_copied = sem("gk_copied")
        gv_copied = sem("gv_copied")
        gq_copied = sem("gq_copied")
        gr_ready = sem("gr_ready")
        kdec_ready = sem("kdec_ready")
        upd_ready = sem("upd_ready")
        state_ready = sem("state_ready")
        go_ready = sem("go_ready")
        go_copied = sem("go_copied")
        go_sq = sem("go_sq")
        go_sums = sem("go_sums")
        go_mean = sem("go_mean")
        go_var = sem("go_var")
        go_std = sem("go_std")
        go_h = sem("go_h")
        tapped = sem("tapped")
        up_conv = sem("up_conv")
        go_sub = sem("go_sub")
        go_mul = sem("go_mul")
        meta_lo = sem("meta_lo")
        cg_copied = sem("cg_copied")
        hc_ready = sem("hc_ready")
        ks_copied = sem("ks_copied")
        vT_copied = sem("vT_copied")
        vt_turned = sem("vt_turned")
        vs_copied = sem("vs_copied")
        f_logit = sem("f_logit")
        f_ln = sem("f_ln")
        c_ready = sem("c_ready")
        cq_ready = sem("cq_ready")
        cq_copied = sem("cq_copied")
        aq_copied = sem("aq_copied")

        cols_of = {name: slice(0, T) if name in ("ffn2", "conv", "ffn3") else TOK for name in LN}

        def each_unit(eng, phase, body, n=None, first=0):
            n = n or dict(PHASES)[phase]
            base = BASE[phase] + first
            turns = n // RING - (base + n + RING > UNITS)
            if turns < 2:
                turns = 0
            else:
                with eng.Fori(0, turns) as it:
                    for r in range(RING):
                        body(base + RING * it + r, (base + r) % RING, RING * it + r, 2 * it + r // 2, r)
            for i in range(RING * turns, n):
                body(base + i, (base + i) % RING, i, i // 2, i % RING)

        block = ctx.enter_context(nc.Block())

        @block.sync
        def _(sp):
            def load(u, slot):
                sp.dma_start(raw[:, slot, :], stream[bass.ds(u, 1), :, :].rearrange("a p n -> p (a n)")
                             ).then_inc(w_landed[slot], 16)

            for u in range(RING):
                load(u, u)
            turns = UNITS // RING - 1
            with sp.Fori(0, turns) as it:
                for r in range(RING):
                    sp.wait_ge(w_lo_ready, RING * it + r + 1)
                    load(RING * it + RING + r, r)
            for u in range(RING * (turns + 1), UNITS):
                sp.wait_ge(w_lo_ready, u - RING + 1)
                load(u, u % RING)
            for n in range(KD):
                sp.wait_ge(x_ready, 9 * KD + n + 1)
                sp.dma_start(out[n * P:(n + 1) * P, :], x[:, n, TOK]).then_inc(out_done, 16)
            sp.wait_ge(out_done, 16 * KD)

        @block.scalar
        def _(act):
            def hi(u, slot):
                if isinstance(u, int) and u >= UNITS:
                    return
                act.wait_ge(w_landed[slot], (u - slot) * 4 + 16)
                if not (isinstance(u, int) and u < RING):
                    act.wait_ge(unit_done, u - RING + 1)
                nc.scalar.activation(w_hi[:, slot, :], raw[:, slot, :], ACT.Copy).then_inc(w_hi_ready, 1)

            steps = [0]

            def link(ins):
                steps[0] += 1
                ins.then_inc(act_step, 1)
                act.wait_ge(act_step, steps[0])

            def squares(k, tiles, cols):
                for n in tiles:
                    act.wait_ge(y_ready, KD * k + n + 1)
                    nc.scalar.activation(sq[:, n, cols], y[:, n, cols], ACT.Square).then_inc(sq_ready, 1)

            def layer_norm(k, cols):
                n_cols = cols.stop - cols.start
                act.wait_ge(stats_ready, k + 1)
                nc.scalar.activation(mu[:, cols], ps[:, 6, 0:n_cols], ACT.Copy, scale=1.0 / D).then_inc(mean_ready, 1)
                nc.scalar.activation(var[:, cols], ps[:, 6, 0:n_cols], ACT.Square, scale=1.0 / D).then_inc(mean_ready, 1)
                act.wait_ge(var_ready, k + 1)
                nc.scalar.activation(var[:, cols], var[:, cols], ACT.Sqrt).then_inc(std_ready, 1)
                for n in range(KD + 1):
                    if n < KD:
                        act.wait_ge(normed, KD * k + n + 1)
                        nc.scalar.activation(x[:, n, cols], y[:, n, cols], ACT.Identity, scale=pcol("ln_g", KD * k + n),
                                             bias=pcol("ln_b", KD * k + n)).then_inc(x_ready, 1)
                    if n > 0 and k < 9:
                        act.wait_ge(x_ready, KD * k + n)
                        nc.scalar.activation(a_hi[:, n - 1, cols], x[:, n - 1, cols], ACT.Copy).then_inc(x_hi_ready, 1)

            def attention(first, n_heads, h_base, w0, w1, sm, pt, ptm):
                for t in range(n_heads + 1):
                    if t < n_heads:
                        a = first + t
                        at = 4 * (a % 2)
                        act.wait_ge(maxed, a + 1)
                        for b, part in ((0, slice(0, w0)), (1, slice(w0, w0 + w1))):
                            nc.scalar.activation(sm[:, a % 2, part], sm[:, a % 2, part], ACT.Exp,
                                                 bias=cols[:, at + b:at + b + 1],
                                                 accum_out=cols[:, at + 2 + b:at + 3 + b]).then_inc(exped, 1)
                    if t > 0:
                        a = first + t - 1
                        act.wait_ge(turned, a + 1)
                        nc.scalar.activation(pt[:, :], ps[:, 6, 0:384], ACT.Copy).then_inc(turned_sb, 1)
                        if ptm is not None:
                            nc.scalar.activation(ptm[0:META, :], ps[0:META, 7, 256:512], ACT.Copy).then_inc(turned_sb, 1)
                        act.wait_ge(mixed, a + 1)
                        nc.scalar.activation(h_hi[:, h_base + t - 1, TOK], ps[:, 7, 0:SEQ], ACT.Copy).then_inc(h_hi_ready, 1)

            def ffn(f):
                cw = ffn_cols(f)
                n_cols = cw.stop - cw.start
                conv = f in CONV_FFNS

                def up(u, slot, i, j, r):
                    jb = r // 2
                    hi(u + RING, slot)
                    if conv:
                        tap, done = ((f_tg, gate_tap), (f_tu, up_tap))[r % 2]
                        nc.scalar.activation(tap[:, jb, 0:n_cols], ps[:, slot, 0:n_cols], ACT.Identity,
                                             scale=par[:, bass.ds(COL["conv_w"] + (3 * f + 2) * 2 * NF + i, 1)],
                                             bias=par[:, bass.ds(COL["conv_b"] + f * 2 * NF + i, 1)]).then_inc(done, 1)
                        if r % 2 == 0:
                            act.wait_ge(gate_conv, f * NF + j + 1)
                            nc.scalar.activation(f_act[:, jb, 0:n_cols], f_tg[:, jb, 0:n_cols],
                                                 ACT.Gelu_apprx_tanh).then_inc(gated, 1)
                    elif r % 2 == 0:
                        nc.scalar.activation(f_act[:, jb, 0:n_cols], ps[:, slot, 0:n_cols], ACT.Silu).then_inc(gated, 1)
                    if r % 2 == 1:
                        act.wait_ge(h_ready, f * NF + j + 1)
                        nc.scalar.activation(cols[0:1, 60:61], par[0:1, 0:1], ACT.Copy)
                        nc.scalar.activation(h_hi[:, bass.ds(j, 1), cw], f_h[:, jb:jb + 1, 0:n_cols],
                                             ACT.Copy).then_inc(h_hi_ready, 1)

                def down(u, slot, i, j, r):
                    hi(u + RING, slot)

                each_unit(act, f"up{f}", up)
                each_unit(act, f"down{f}", down, 11)
                squares(LN[f"ffn{f}"], range(4), cw)
                each_unit(act, f"down{f}", down, 11, 11)
                squares(LN[f"ffn{f}"], range(4, 8), cw)

            def embedding(l):
                u = BASE[f"proj{l}"]
                for i in range(2):
                    slot = (u + i) % RING
                    act.wait_ge(unit_done, u + i + 1)
                    nc.scalar.activation(pp[:, 4 * i:4 * i + 2, :].rearrange("p a b -> p (a b)"), ps[:, slot, :],
                                         ACT.Copy).then_inc(pp_copied, 1)
                    nc.scalar.activation(pp[:, 4 * i + 2:4 * i + 4, :].rearrange("p a b -> p (a b)"), ps[:, 4 + i, :],
                                         ACT.Copy).then_inc(pp_copied, 1)
                    hi(u + i + RING, slot)
                u = BASE[f"gate{l}"]
                for n in range(KD):
                    slot = (u + n) % RING
                    act.wait_ge(unit_done, u + n + 1)
                    nc.scalar.activation(f_act[:, n % 2, 0:SEQ], ps[:, slot, 0:SEQ], ACT.Sigmoid,
                                         bias=pcol("ple_b", KD * l + n)).then_inc(sig_ready, 1)
                    hi(u + n + RING, slot)
                    act.wait_ge(px_ready, KD * l + n + 1)
                    nc.scalar.activation(b_hi[:, n, TOK], x[:, n, TOK], ACT.Copy).then_inc(x_hi_ready, 1)

            def load_p(l):
                act.dma_start(p_raw, pT[l].rearrange("(k p) t -> p k t", p=P)).then_inc(in_p, 16)

            def split_p(l):
                act.wait_ge(in_p, 16 * (l + 1))
                act.wait_ge(unit_done, BASE[f"proj{l}"])
                for n in range(2):
                    nc.scalar.activation(h_hi[:, n, TOK], p_raw[:, n, :], ACT.Copy).then_inc(p_hi, 1)

            def plain(phase, k, cw, per=1):
                for i in range(dict(PHASES)[phase]):
                    u = BASE[phase] + i
                    hi(u + RING, u % RING)
                    if i % per == per - 1:
                        squares(k, [i // per], cw)

            for n in range(KD):
                act.dma_start(x[:, n, TOK], xT[n * P:(n + 1) * P, :]).then_inc(in_x, 16)
            act.dma_start(par[:, :], params).then_inc(in_par, 16)
            act.dma_start(con[:, :], consts).then_inc(in_con, 16)
            act.dma_start(x[:, :, 0:META], metaT.rearrange("(k p) t -> p k t", p=P)).then_inc(in_meta, 16)
            act.dma_start(posi, pos.partition_broadcast(P).rearrange("q a t -> q (a t)")).then_inc(in_pos, 16)
            for b in range(2):
                act.dma_start(icol[:, b:b + 1], pos[0, b * P:(b + 1) * P].rearrange("(p a) -> p a", a=1)).then_inc(in_pos, 16)
            act.wait_ge(in_x, 16 * KD)
            for n in range(KD):
                nc.scalar.activation(a_hi[:, n, TOK], x[:, n, TOK], ACT.Copy).then_inc(x_hi_ready, 1)
            for u in range(RING):
                hi(u, u)
            act.wait_ge(in_meta, 16)
            nc.scalar.activation(b_hi[:, :, 0:META], x[:, :, 0:META], ACT.Copy).then_inc(meta_split, 1)
            act.wait_ge(rope_arg, 1)
            nc.scalar.activation(sinT, sinT, ACT.Sin).then_inc(rope_tab, 1)
            nc.scalar.activation(cosT, cosT, ACT.Sin).then_inc(rope_tab, 1)

            u = BASE["mla_in"]
            for n in range(7):
                act.wait_ge(unit_done, u + n + 1)
                if n < 6:
                    nc.scalar.activation(c_raw[:, n, :], ps[:, (u + n) % RING, 0:SEQ], ACT.Copy).then_inc(c_copied, 1)
                    nc.scalar.activation(c_sq[:, n, :], ps[:, (u + n) % RING, 0:SEQ], ACT.Square).then_inc(c_copied, 1)
                else:
                    nc.scalar.activation(kr_raw, ps[:, (u + n) % RING, 0:SEQ], ACT.Copy).then_inc(c_copied, 1)
                hi(u + n + RING, (u + n) % RING)
            act.wait_ge(c_var, 2)
            nc.scalar.activation(c_rstd, c_rstd, ACT.Sqrt).then_inc(c_std, 1)
            for n in range(6):
                act.wait_ge(c_normed, n + 1)
                nc.scalar.activation(b_hi[:, n, TOK], c_raw[:, n, :], ACT.Copy).then_inc(c_hi, 1)
            for half in range(2):
                for phase, n, what in (("mla_qn", 4, "qn"), ("mla_qr", 2, "qr"), ("mla_kn", 2, "kn"), ("mla_v", 2, "v")):
                    for i in range(n):
                        u = BASE[f"{phase}{half}"] + i
                        slot = u % RING
                        act.wait_ge(unit_done, u + 1)
                        if what == "qn":
                            nc.scalar.activation(qn[:, 2 * i:2 * i + 2, :].rearrange("p a b -> p (a b)"), ps[:, slot, :],
                                                 ACT.Copy).then_inc(q_copied, 1)
                        elif what == "qr":
                            nc.scalar.activation(qr_raw[:, 2 * i:2 * i + 2, :].rearrange("p a b -> p (a b)"),
                                                 ps[:, slot, :], ACT.Copy).then_inc(qr_copied, 1)
                        elif what == "kn":
                            for b, bank in enumerate((slot, 6 + i)):
                                nc.scalar.activation(
                                    kn[:, 4 * i + 2 * b:4 * i + 2 * b + 2, :].rearrange("p a b -> p (a b)"),
                                    ps[:, bank, :], ACT.Copy).then_inc(k_copied, 1)
                        else:
                            for m, bank in enumerate((slot, 4 + i)):
                                nc.scalar.activation(vm[:, m, 512 * i:512 * i + 512], ps[:, bank, :],
                                                     ACT.Copy).then_inc(v_copied, 1)
                        hi(u + RING, slot)
                attention(8 * half, 8, 8 * half, 128, 256, sm_m, pt_m, None)
            plain("mla_o", LN["mla"], TOK, 2)
            layer_norm(LN["mla"], TOK)

            load_p(0)
            ffn(0)
            split_p(0)
            layer_norm(LN["ffn0"], TOK)
            embedding(0)

            act.dma_start(g_wa2[0:32, :], wa2).then_inc(in_wa2, 16)
            u = BASE["gla_a"]
            act.wait_ge(unit_done, u + 1)
            nc.scalar.activation(g_aT[0:32, :], ps[0:32, u % RING, 0:SEQ], ACT.Identity,
                                 bias=ccol("one16")[0:32, :]).then_inc(aT_ready, 1)
            hi(u + RING, u % RING)
            for i in range(4):
                u = BASE["gla_k"] + i
                hi(u + RING, u % RING)
            act.wait_ge(unit_done, BASE["gla_v"])
            for m in range(2):
                nc.scalar.activation(g_k[:, m, :], ps[:, m, :], ACT.Copy).then_inc(gk_copied, 1)
            u = BASE["gla_v"]
            hi(u + RING, u % RING)
            act.wait_ge(z_ready, 1)
            nc.scalar.activation(g_t[:, 0, :], ps[:, 6, :], ACT.Abs)
            link(nc.scalar.activation(g_t[:, 1, :], ps[:, 7, :], ACT.Abs))
            link(nc.scalar.activation(g_t, g_t, ACT.Exp, scale=-1.0))
            nc.scalar.activation(g_t, g_t, ACT.Ln, bias=1.0).then_inc(ln_ready, 1)
            for i in range(1, 4):
                hi(u + i + RING, (u + i) % RING)
            act.wait_ge(unit_done, u + 4)
            for m in range(2):
                nc.scalar.activation(g_v[:, m, 0:512], ps[:, 2 + m, :], ACT.Copy).then_inc(gv_copied, 1)
            act.wait_ge(suf_ready, 1)
            for m in range(2):
                nc.scalar.activation(g_ed[:, m, :], ps[:, 6 + m, :], ACT.Exp, scale=1.0 / GLA_TAU).then_inc(ed_ready, 1)
            act.wait_ge(tot_ready, 1)
            nc.scalar.activation(g_dec.rearrange("p a b -> p (a b)"), ps[:, 4, 0:16], ACT.Exp,
                                 scale=1.0 / GLA_TAU).then_inc(dec_ready, 1)
            for i in range(4, 8):
                hi(u + i + RING, (u + i) % RING)
            act.wait_ge(unit_done, u + 8)
            for m in range(2):
                nc.scalar.activation(g_v[:, m, 512:1024], ps[:, m, :], ACT.Copy).then_inc(gv_copied, 1)
            for i in range(4):
                u = BASE["gla_q"] + i
                act.wait_ge(unit_done, u + 1)
                nc.scalar.activation(g_q[:, i, :], ps[:, u % RING, 0:SEQ], ACT.Copy, scale=GLA_SCALE).then_inc(gq_copied, 1)
                hi(u + RING, u % RING)
            for n in range(8):
                u = BASE["gla_r"] + n
                act.wait_ge(unit_done, u + 1)
                nc.scalar.activation(g_rs[:, n, :], ps[:, u % RING, 0:SEQ], ACT.Silu).then_inc(gr_ready, 1)
                hi(u + RING, u % RING)
                if n % 2 == 1:
                    c = n // 2
                    act.wait_ge(go_ready, c + 1)
                    nc.scalar.activation(g_o[:, :, CHUNK * c:CHUNK * (c + 1)],
                                         ps[:, 6 + c % 2, :].rearrange("p (a b) -> p a b", a=8), ACT.Copy).then_inc(go_copied, 1)
            act.wait_ge(go_copied, 4)
            nc.scalar.activation(g_osq, g_o, ACT.Square).then_inc(go_sq, 1)
            act.wait_ge(go_sums, 1)
            for b in range(2):
                two = slice(2 * b, 2 * b + 2)
                nc.scalar.activation(g_mu[:, two, :].rearrange("p a b -> p (a b)"), ps[:, 4 + b, :], ACT.Copy,
                                     scale=1.0 / 256).then_inc(go_mean, 1)
                nc.scalar.activation(g_var[:, two, :].rearrange("p a b -> p (a b)"), ps[:, 4 + b, :], ACT.Square,
                                     scale=1.0 / 256).then_inc(go_mean, 1)
            act.wait_ge(go_var, 1)
            nc.scalar.activation(g_var, g_var, ACT.Sqrt).then_inc(go_std, 1)
            for t in range(8):
                act.wait_ge(go_h, t + 1)
                nc.scalar.activation(h_hi[:, t, TOK], g_h[:, t % 2, :], ACT.Copy).then_inc(h_hi_ready, 1)
            plain("gla_o", LN["gla"], TOK)
            layer_norm(LN["gla"], TOK)

            load_p(1)
            ffn(1)
            split_p(1)
            layer_norm(LN["ffn1"], TOK)
            embedding(1)

            ffn(2)
            layer_norm(LN["ffn2"], slice(0, T))
            for i in range(24):
                u, n = BASE["conv_in"] + i, i // 3
                act.wait_ge(unit_done, u + 1)
                if i % 3 == 0:
                    nc.scalar.activation(f_tg[:, n % 2, :], ps[:, u % RING, 0:T], ACT.Copy).then_inc(cg_copied, 1)
                hi(u + RING, u % RING)
                if i % 3 == 2:
                    act.wait_ge(hc_ready, n + 1)
                    nc.scalar.activation(h_hi[:, n, :], f_h[:, n % 2, :], ACT.Copy).then_inc(h_hi_ready, 1)
            plain("conv_out", LN["conv"], slice(0, T))
            layer_norm(LN["conv"], slice(0, T))
            ffn(3)
            layer_norm(LN["ffn3"], slice(0, T))
            for n in range(8):
                u = BASE["kv_k"] + n
                act.wait_ge(unit_done, u + 1)
                nc.scalar.activation(k_sh[:, n, :], ps[:, u % RING, 0:T], ACT.Copy).then_inc(ks_copied, 1)
                hi(u + RING, u % RING)
            for n in range(8):
                u = BASE["kv_v"] + n
                act.wait_ge(unit_done, u + 1)
                if n >= 2:
                    act.wait_ge(vt_turned, n - 1)
                nc.scalar.activation(vT[:, n % 2, :], ps[:, u % RING, 0:T], ACT.Copy).then_inc(vT_copied, 1)
                hi(u + RING, u % RING)
            u = BASE["kv_f"]
            act.wait_ge(unit_done, u + 1)
            nc.scalar.activation(f_z[0:8, :], ps[0:8, u % RING, 0:T], ACT.Identity, bias=pcol("f_bias")[0:8, :]).then_inc(f_logit, 1)
            link(nc.scalar.activation(f_t[0:8, :], ps[0:8, u % RING, 0:T], ACT.Abs, bias=pcol("f_bias")[0:8, :]))
            link(nc.scalar.activation(f_t[0:8, :], f_t[0:8, :], ACT.Exp, scale=-1.0))
            nc.scalar.activation(f_t[0:8, :], f_t[0:8, :], ACT.Ln, bias=1.0).then_inc(f_ln, 1)
            hi(u + RING, u % RING)

            ffn(4)
            layer_norm(LN["ffn4"], TOK)
            act.dma_start(mask_a, causal).then_inc(in_causal, 16)
            for n in range(8):
                u = BASE["att_q"] + n
                act.wait_ge(unit_done, u + 1)
                nc.scalar.activation(a_q[:, n, :], ps[:, u % RING, 0:SEQ], ACT.Copy, scale=ATT_SCALE).then_inc(aq_copied, 1)
                hi(u + RING, u % RING)
            attention(16, 8, 0, 144, 272, sm_a, pt_a, ptm_a)
            plain("att_o", LN["att"], TOK)
            layer_norm(LN["att"], TOK)
            ffn(5)
            layer_norm(LN["ffn5"], TOK)

        @block.gpsimd
        def _(pool):
            steps = [0]

            def sums(k, tiles, cw):
                for n in range(1, tiles):
                    pool.wait_ge(y_ready, KD * k + n + 1)
                    pool.wait_ge(sq_ready, KD * k + n + 1)
                    last = n == tiles - 1
                    for acc, src in ((acc1, y), (acc2, sq)):
                        first = src[:, 0, cw] if n == 1 else acc[:, cw]
                        ins = nc.gpsimd.tensor_tensor(acc[:, cw], first, src[:, n, cw], ALU.add)
                        ins.then_inc(sums_ready if last else pool_step, 1)
                    if not last:
                        steps[0] += 2
                        pool.wait_ge(pool_step, steps[0])

            for name, k in LN.items():
                sums(k, 4 if name.startswith("ffn") else 6, cols_of[name])

        @block.vector
        def _(dve):
            def lo(u, slot):
                if isinstance(u, int) and u >= UNITS:
                    return
                dve.wait_ge(w_hi_ready, u + 1)
                nc.vector.tensor_tensor(w_lo[:, slot, :], raw[:, slot, :], w_hi[:, slot, :].bitcast(F32),
                                        ALU.subtract).then_inc(w_lo_ready, 1)

            def lo_next(u):
                lo(u + RING - 1, (u + RING - 1) % RING)

            steps = [0]

            def link(*ins):
                steps[0] += 1
                ins[-1].then_inc(dve_step, 1)
                dve.wait_ge(dve_step, steps[0])

            def residual(k, n, bank, cw):
                nc.vector.scalar_tensor_tensor(y[:, n, cw], x[:, n, cw], ALPHA, ps[:, bank, 0:cw.stop - cw.start],
                                               ALU.mult, ALU.add).then_inc(y_ready, 1)

            def layer_norm(k, cw, split):
                n_cols = cw.stop - cw.start
                dve.wait_ge(mean_ready, 2 * k + 2)
                link(nc.vector.scalar_tensor_tensor(var[:, cw], ps[:, 7, 0:n_cols], 1.0 / D, var[:, cw],
                                                    ALU.mult, ALU.subtract))
                nc.vector.tensor_scalar(var[:, cw], var[:, cw], 0.0, EPS, ALU.max, ALU.add).then_inc(var_ready, 1)
                dve.wait_ge(std_ready, k + 1)
                link(nc.vector.reciprocal(var[:, cw], var[:, cw]))
                for n in range(KD + 3):
                    if n < KD:
                        nc.vector.tensor_tensor(y[:, n, cw], y[:, n, cw], mu[:, cw], ALU.subtract).then_inc(dve_step, 1)
                    if 0 < n <= KD:
                        dve.wait_ge(dve_step, steps[0] + n)
                        nc.vector.tensor_tensor(y[:, n - 1, cw], y[:, n - 1, cw], var[:, cw], ALU.mult).then_inc(normed, 1)
                    if n >= 3 and k < 9:
                        m = n - 3
                        dve.wait_ge(x_hi_ready, X_SPLIT[split] + m + 1)
                        nc.vector.tensor_tensor(a_lo[:, m, cw], x[:, m, cw], a_hi[:, m, cw].bitcast(F32),
                                                ALU.subtract).then_inc(x_split, 1)
                steps[0] += KD

            def attention(first, n_heads, h_base, h_tile, w0, w1, sm, mask, mla):
                for t in range(n_heads + 2):
                    if t < n_heads:
                        a = first + t
                        at, bank = 4 * (a % 2), 4 + a % 2
                        dve.wait_ge(scores, a + 1)
                        if t >= 2:
                            dve.wait_ge(turned, a - 1)
                        if mla:
                            link(nc.vector.scalar_tensor_tensor(sm[:, a % 2, :], ps[:, bank, 0:w0 + w1], MLA_SCALE, mask,
                                                                ALU.mult, ALU.add))
                        else:
                            nc.vector.scalar_tensor_tensor(sm[:, a % 2, 0:w0], ps[:, bank, 0:w0],
                                                           cq_col[:, 0, t:t + 1], mask[:, 0:w0], ALU.add, ALU.add)
                            link(nc.vector.scalar_tensor_tensor(sm[:, a % 2, w0:w0 + w1], ps[:, bank, w0:w0 + w1],
                                                                cq_col[:, 1, t:t + 1], mask[:, w0:w0 + w1],
                                                                ALU.add, ALU.add))
                        nc.vector.tensor_reduce(cols[:, at:at + 1], sm[:, a % 2, 0:w0], AX_X, ALU.max, negate=True)
                        nc.vector.tensor_reduce(cols[:, at + 1:at + 2], sm[:, a % 2, w0:w0 + w1], AX_X, ALU.max,
                                                negate=True).then_inc(maxed, 1)
                    if 0 < t <= n_heads:
                        a = first + t - 1
                        at = 4 * (a % 2)
                        dve.wait_ge(exped, 2 * a + 2)
                        link(nc.vector.reciprocal(cols[:, 8 + at:10 + at], cols[:, at + 2:at + 4]))
                        nc.vector.tensor_scalar(sm[:, a % 2, 0:w0], sm[:, a % 2, 0:w0], cols[:, 8 + at:9 + at], None, ALU.mult)
                        nc.vector.tensor_scalar(sm[:, a % 2, w0:w0 + w1], sm[:, a % 2, w0:w0 + w1],
                                                cols[:, 9 + at:10 + at], None, ALU.mult).then_inc(probs, 1)
                    if t >= 2:
                        n = h_tile + t - 2
                        dve.wait_ge(h_hi_ready, h_base + t - 1)
                        nc.vector.tensor_tensor(h_lo[:, n, TOK], ps[:, 7, 0:SEQ], h_hi[:, n, TOK].bitcast(F32),
                                                ALU.subtract).then_inc(h_split, 1)

            def ffn(f):
                cw = ffn_cols(f)
                n_cols = cw.stop - cw.start
                conv = f in CONV_FFNS
                base = H_SPLIT[f"ffn{f}"]

                def taps(t, jb, slot, i, dve_count):
                    w = COL["conv_w"] + 3 * f * 2 * NF
                    nc.vector.scalar_tensor_tensor(t[:, jb, 1:SEQ], ps[:, slot, 0:SEQ - 1],
                                                   par[:, bass.ds(w + 2 * NF + i, 1)], t[:, jb, 1:SEQ],
                                                   ALU.mult, ALU.add).then_inc(tapped, 1)
                    dve.wait_ge(tapped, dve_count)
                    return nc.vector.scalar_tensor_tensor(t[:, jb, 2:SEQ], ps[:, slot, 0:SEQ - 2],
                                                          par[:, bass.ds(w + i, 1)], t[:, jb, 2:SEQ], ALU.mult, ALU.add)

                def up(u, slot, i, j, r):
                    jb = r // 2
                    if r % 2 == 0:
                        lo(u + RING - 1, (slot + RING - 1) % RING)
                        if conv:
                            dve.wait_ge(gate_tap, f * NF + j + 1)
                            taps(f_tg, jb, slot, i, f * 2 * NF + i + 1).then_inc(gate_conv, 1)
                        return
                    if conv:
                        dve.wait_ge(up_tap, f * NF + j + 1)
                        taps(f_tu, jb, slot, i, f * 2 * NF + i + 1).then_inc(up_conv, 1)
                        dve.wait_ge(gated, f * NF + j + 1)
                        dve.wait_ge(up_conv, f * NF + j + 1)
                        nc.vector.tensor_tensor(f_h[:, jb, 0:n_cols], f_tu[:, jb, 0:n_cols], f_act[:, jb, 0:n_cols],
                                                ALU.mult).then_inc(h_ready, 1)
                    else:
                        dve.wait_ge(unit_done, u + 1)
                        dve.wait_ge(gated, f * NF + j + 1)
                        nc.vector.scalar_tensor_tensor(f_h[:, jb, 0:n_cols], ps[:, slot, 0:n_cols], 0.5,
                                                       f_act[:, jb, 0:n_cols], ALU.mult, ALU.mult).then_inc(h_ready, 1)
                    lo(u + RING - 1, (slot + RING - 1) % RING)
                    dve.wait_ge(h_hi_ready, base + j + 1)
                    nc.vector.tensor_tensor(h_lo[:, bass.ds(j, 1), cw], f_h[:, jb:jb + 1, 0:n_cols],
                                            h_hi[:, bass.ds(j, 1), cw].bitcast(F32), ALU.subtract).then_inc(h_split, 1)

                def down(u, slot, i, j, r):
                    lo(u + RING - 1, (slot + RING - 1) % RING)

                each_unit(dve, f"up{f}", up)
                each_unit(dve, f"down{f}", down, 11)
                for half in range(2):
                    dve.wait_ge(unit_done, BASE[f"down{f}"] + 11 * (half + 1))
                    for n in range(4):
                        residual(LN[f"ffn{f}"], 4 * half + n, (4 if half == 0 else 0) + n, cw)
                    if half == 0:
                        each_unit(dve, f"down{f}", down, 11, 11)

            def embedding(l):
                for i in range(2):
                    lo_next(BASE[f"proj{l}"] + i)
                dve.wait_ge(pp_copied, 4 * (l + 1))
                u = BASE[f"gate{l}"]
                for n in range(KD):
                    dve.wait_ge(sig_ready, KD * l + n + 1)
                    link(nc.vector.tensor_tensor(f_act[:, n % 2, 0:SEQ], f_act[:, n % 2, 0:SEQ], pp[:, n, :], ALU.mult))
                    nc.vector.tensor_tensor(x[:, n, TOK], x[:, n, TOK], f_act[:, n % 2, 0:SEQ], ALU.add).then_inc(px_ready, 1)
                    lo_next(u + n)
                    dve.wait_ge(x_hi_ready, X_SPLIT[f"ple{l}"] + n + 1)
                    nc.vector.tensor_tensor(b_lo[:, n, TOK], x[:, n, TOK], b_hi[:, n, TOK].bitcast(F32),
                                            ALU.subtract).then_inc(x_split, 1)

            def values(n):
                dve.wait_ge(vt_turned, n + 1)
                nc.vector.tensor_copy(v_sh[0:META, 0, n * P:(n + 1) * P], ps[0:META, 4 + n % 2, 0:P]).then_inc(vs_copied, 1)
                nc.vector.tensor_copy(v_sh[:, 1:3, n * P:(n + 1) * P],
                                      ps[:, 4 + n % 2, P:3 * P].rearrange("p (a b) -> p a b", a=2)).then_inc(vs_copied, 1)

            def split_p(l):
                for n in range(2):
                    dve.wait_ge(p_hi, 2 * l + n + 1)
                    nc.vector.tensor_tensor(h_lo[:, n, TOK], p_raw[:, n, :], h_hi[:, n, TOK].bitcast(F32),
                                            ALU.subtract).then_inc(p_split, 1)

            def plain(phase, k, cw, per=1):
                n_units = dict(PHASES)[phase]
                for i in range(n_units):
                    u = BASE[phase] + i
                    if i % per == per - 1:
                        dve.wait_ge(unit_done, u + 1)
                        residual(k, i // per, (u - per + 1) % RING, cw)
                    lo_next(u)

            nc.vector.memset(ones[:, :], 1.0).then_inc(zeroed, 1)
            nc.vector.memset(krm.rearrange("p a b -> p (a b)"), 0.0).then_inc(zeroed, 1)
            dve.wait_ge(in_x, 16 * KD)
            for n in range(KD):
                dve.wait_ge(x_hi_ready, n + 1)
                nc.vector.tensor_tensor(a_lo[:, n, TOK], x[:, n, TOK], a_hi[:, n, TOK].bitcast(F32),
                                        ALU.subtract).then_inc(x_split, 1)
            for u in range(RING - 1):
                lo(u, u)
            dve.wait_ge(in_con, 16)
            dve.wait_ge(in_pos, 48)
            link(nc.vector.tensor_copy(posf, posi))
            link(nc.vector.tensor_scalar(cosT, posf, ccol("inv_freq"), None, ALU.mult))
            link(nc.vector.tensor_scalar(rope_a, cosT, float(1 / TWO_PI), MAGIC, ALU.mult, ALU.add))
            link(nc.vector.tensor_scalar(rope_a, rope_a, -MAGIC, None, ALU.add))
            for part in (6.28125, 1.93500518798828125e-3, float(TWO_PI - 6.28125 - 1.93500518798828125e-3)):
                link(nc.vector.scalar_tensor_tensor(cosT, rope_a, -part, cosT, ALU.mult, ALU.add))
            link(nc.vector.tensor_scalar(sinT, cosT, 3.1415925, -3.1415925, ALU.min, ALU.max))
            link(nc.vector.tensor_scalar(rope_b, cosT, float(np.pi / 2), float(TWO_PI), ALU.is_gt, ALU.mult))
            link(nc.vector.scalar_tensor_tensor(cosT, cosT, float(np.pi / 2), rope_b, ALU.add, ALU.subtract))
            nc.vector.tensor_scalar(cosT, cosT, 3.1415925, -3.1415925, ALU.min, ALU.max).then_inc(rope_arg, 1)
            link(nc.vector.tensor_scalar(posi, posi, 6, None, ALU.arith_shift_right))
            link(nc.vector.tensor_scalar(icol[:, 2:4], icol[:, 0:2], 6, None, ALU.arith_shift_right))
            nc.vector.tensor_copy(posf, posi)
            link(nc.vector.tensor_copy(cols[:, 40:42], icol[:, 2:4]))
            nc.vector.tensor_scalar(mask_m[:, 0:P], posf[:, 0:P], cols[:, 40:41], NEG, ALU.is_gt, ALU.mult)
            link(nc.vector.tensor_scalar(mask_m[:, P:384], posf, cols[:, 41:42], NEG, ALU.is_gt, ALU.mult))
            dve.wait_ge(rope_tab, 2)
            link(nc.vector.tensor_scalar(sinT, sinT, ccol("rope_sign"), None, ALU.mult))
            dve.wait_ge(meta_split, 1)
            nc.vector.tensor_tensor(b_lo[:, :, 0:META], x[:, :, 0:META], b_hi[:, :, 0:META].bitcast(F32),
                                    ALU.subtract).then_inc(meta_lo, 1)

            u = BASE["mla_in"]
            for n in range(7):
                lo_next(u + n)
            dve.wait_ge(c_sums, 1)
            nc.vector.tensor_scalar(c_rstd[:, 0, :], ps[:, 6, 0:SEQ], 1.0 / 512, EPS, ALU.mult, ALU.add).then_inc(c_var, 1)
            nc.vector.tensor_scalar(c_rstd[:, 1, :], ps[:, 6, SEQ:512], 1.0 / 256, EPS, ALU.mult, ALU.add).then_inc(c_var, 1)
            dve.wait_ge(c_std, 1)
            link(nc.vector.reciprocal(c_rstd, c_rstd))
            for n in range(7):
                if n < 6:
                    g = pcol("q_norm", n) if n < 4 else pcol("kv_norm", n - 4)
                    nc.vector.scalar_tensor_tensor(c_raw[:, n, :], c_raw[:, n, :], g, c_rstd[:, n // 4, :],
                                                   ALU.mult, ALU.mult).then_inc(c_normed, 1)
                if n > 0:
                    dve.wait_ge(c_hi, n)
                    nc.vector.tensor_tensor(b_lo[:, n - 1, TOK], c_raw[:, n - 1, :], b_hi[:, n - 1, TOK].bitcast(F32),
                                            ALU.subtract).then_inc(c_split, 1)
            dve.wait_ge(kr_swapped, 1)
            dve.wait_ge(c_copied, 13)
            dve.wait_ge(c_split, 6)
            nc.vector.tensor_tensor(kr_raw, kr_raw, cosT, ALU.mult)
            link(nc.vector.tensor_tensor(qr_t[:, 0, :], ps[:, 7, 0:SEQ], sinT, ALU.mult))
            dve.wait_ge(zeroed, 2)
            nc.vector.tensor_tensor(krm[0:64, 0, :], kr_raw[0:64, :], qr_t[0:64, 0, :], ALU.add).then_inc(kr_ready, 1)
            nc.vector.tensor_tensor(krm[64:P, 1, :], kr_raw[64:P, :], qr_t[64:P, 0, :], ALU.add).then_inc(kr_ready, 1)
            for half in range(2):
                for i in range(4):
                    lo_next(BASE[f"mla_qn{half}"] + i)
                for i in range(2):
                    lo_next(BASE[f"mla_qr{half}"] + i)
                for i in range(2):
                    dve.wait_ge(qr_swapped, 2 * half + i + 1)
                    for n in (2 * i, 2 * i + 1):
                        at = (n % 2) * SEQ
                        nc.vector.tensor_tensor(qr_t[:, n, :], ps[:, 4 + i, at:at + SEQ], sinT, ALU.mult)
                        link(nc.vector.tensor_tensor(qr[:, n, :], qr_raw[:, n, :], cosT, ALU.mult))
                        nc.vector.tensor_tensor(qr[:, n, :], qr[:, n, :], qr_t[:, n, :], ALU.add).then_inc(qr_ready, 1)
                for phase in (f"mla_kn{half}", f"mla_v{half}"):
                    for i in range(2):
                        lo_next(BASE[phase] + i)
                attention(8 * half, 8, H_SPLIT["mla"] + 8 * half, 8 * half, 128, 256, sm_m, mask_m, True)
            plain("mla_o", LN["mla"], TOK, 2)
            layer_norm(LN["mla"], TOK, "ln0")
            ffn(0)
            split_p(0)
            layer_norm(LN["ffn0"], TOK, "ln1")
            embedding(0)

            for i in range(5):
                lo_next(BASE["gla_a"] + i)
            dve.wait_ge(ln_ready, 1)
            for m in range(2):
                nc.vector.scalar_tensor_tensor(g_la[:, m, :], ps[:, 6 + m, :], 0.0, g_t[:, m, :],
                                               ALU.min, ALU.subtract).then_inc(la_ready, 1)
            for i in range(4):
                lo_next(BASE["gla_v"] + i)
            dve.wait_ge(gk_copied, 2)
            dve.wait_ge(ed_ready, 2)
            nc.vector.tensor_tensor(g_k, g_k, g_ed, ALU.mult).then_inc(kdec_ready, 1)
            for i in range(8):
                lo_next(BASE["gla_v"] + 4 + i)
            for n in range(8):
                lo_next(BASE["gla_r"] + n)
                if n % 2 == 0:
                    c = n // 2
                    if c == 0:
                        dve.wait_ge(dec_ready, 1)
                    dve.wait_ge(upd_ready, c + 1)
                    for hd in range(4):
                        u_ps = ps[:, 4 + hd // 2, (hd % 2) * 256:(hd % 2 + 1) * 256]
                        if c == 0:
                            ins = nc.vector.tensor_copy(g_S[:, hd, :], u_ps)
                        else:
                            if hd == 0:
                                dve.wait_ge(go_ready, c)
                                dve.wait_ge(state_ready, c)
                            ins = nc.vector.scalar_tensor_tensor(g_S[:, hd, :], g_S[:, hd, :], g_dec[:, hd, c:c + 1],
                                                                 u_ps, ALU.mult, ALU.add)
                    ins.then_inc(state_ready, 1)
            dve.wait_ge(go_mean, 4)
            for b in range(2):
                two = g_var[:, 2 * b:2 * b + 2, :].rearrange("p a b -> p (a b)")
                nc.vector.scalar_tensor_tensor(two, ps[:, 6 + b, :], 1.0 / 256, two, ALU.mult, ALU.subtract).then_inc(dve_step, 1)
            steps[0] += 2
            dve.wait_ge(dve_step, steps[0])
            nc.vector.tensor_scalar(g_var, g_var, 0.0, EPS, ALU.max, ALU.add).then_inc(go_var, 1)
            dve.wait_ge(go_std, 1)
            link(nc.vector.reciprocal(g_var, g_var))
            dve.wait_ge(go_copied, 4)
            dve.wait_ge(gr_ready, 8)
            for t in range(8 + 4):
                if t < 8:
                    nc.vector.tensor_tensor(g_o[:, t, :], g_o[:, t, :], g_mu[:, t // 2, :], ALU.subtract).then_inc(go_sub, 1)
                if 0 <= t - 1 < 8:
                    n = t - 1
                    dve.wait_ge(go_sub, n + 1)
                    nc.vector.tensor_tensor(g_o[:, n, :], g_o[:, n, :], g_var[:, n // 2, :], ALU.mult).then_inc(go_mul, 1)
                if 0 <= t - 2 < 8:
                    n = t - 2
                    dve.wait_ge(go_mul, n + 1)
                    if n >= 2:
                        dve.wait_ge(h_split, H_SPLIT["gla"] + n - 1)
                    nc.vector.scalar_tensor_tensor(g_h[:, n % 2, :], g_o[:, n, :], pcol("o_norm", n), g_rs[:, n, :],
                                                   ALU.mult, ALU.mult).then_inc(go_h, 1)
                if 0 <= t - 3 < 8:
                    n = t - 3
                    dve.wait_ge(h_hi_ready, H_SPLIT["gla"] + n + 1)
                    nc.vector.tensor_tensor(h_lo[:, n, TOK], g_h[:, n % 2, :], h_hi[:, n, TOK].bitcast(F32),
                                            ALU.subtract).then_inc(h_split, 1)
            plain("gla_o", LN["gla"], TOK)
            layer_norm(LN["gla"], TOK, "ln2")
            ffn(1)
            split_p(1)
            layer_norm(LN["ffn1"], TOK, "ln3")
            embedding(1)

            ffn(2)
            layer_norm(LN["ffn2"], slice(0, T), "ln4")
            for n in range(8):
                u = BASE["conv_in"] + 3 * n
                nb = n % 2
                lo_next(u)
                dve.wait_ge(unit_done, u + 2)
                dve.wait_ge(cg_copied, n + 1)
                link(nc.vector.tensor_tensor(f_tg[:, nb, :], ps[:, (u + 1) % RING, 0:T], f_tg[:, nb, :], ALU.mult))
                lo_next(u + 1)
                link(nc.vector.tensor_scalar(f_tu[:, nb, :], f_tg[:, nb, :], pcol("sconv_w", 16 + n), None, ALU.mult))
                link(nc.vector.scalar_tensor_tensor(f_tu[:, nb, 1:T], f_tg[:, nb, 0:T - 1], pcol("sconv_w", 8 + n),
                                                    f_tu[:, nb, 1:T], ALU.mult, ALU.add))
                link(nc.vector.scalar_tensor_tensor(f_tu[:, nb, 2:T], f_tg[:, nb, 0:T - 2], pcol("sconv_w", n),
                                                    f_tu[:, nb, 2:T], ALU.mult, ALU.add))
                dve.wait_ge(unit_done, u + 3)
                nc.vector.tensor_tensor(f_h[:, nb, :], ps[:, (u + 2) % RING, 0:T], f_tu[:, nb, :], ALU.mult).then_inc(hc_ready, 1)
                lo_next(u + 2)
                dve.wait_ge(h_hi_ready, H_SPLIT["conv"] + n + 1)
                nc.vector.tensor_tensor(h_lo[:, n, :], f_h[:, nb, :], h_hi[:, n, :].bitcast(F32),
                                        ALU.subtract).then_inc(h_split, 1)
            plain("conv_out", LN["conv"], slice(0, T))
            layer_norm(LN["conv"], slice(0, T), "ln5")
            ffn(3)
            layer_norm(LN["ffn3"], slice(0, T), "ln6")
            for n in range(8):
                lo_next(BASE["kv_k"] + n)
            for n in range(8):
                lo_next(BASE["kv_v"] + n)
                if n > 0:
                    values(n - 1)
            lo_next(BASE["kv_f"])
            values(7)
            dve.wait_ge(f_ln, 1)
            dve.wait_ge(f_logit, 1)
            nc.vector.memset(f_one[0:8, :], 1.0)
            link(nc.vector.scalar_tensor_tensor(f_z[0:8, :], f_z[0:8, :], 0.0, f_t[0:8, :], ALU.min, ALU.subtract))
            link(nc.vector.tensor_tensor_scan(cum_c[0:8, :], f_one[0:8, :], f_z[0:8, :], 0.0, ALU.mult, ALU.add))
            nc.vector.tensor_scalar(neg_c[0:8, :], cum_c[0:8, :], -1.0, None, ALU.mult).then_inc(c_ready, 1)
            ffn(4)
            layer_norm(LN["ffn4"], TOK, "ln7")
            for n in range(8):
                lo_next(BASE["att_q"] + n)
            dve.wait_ge(cq_ready, 1)
            nc.vector.tensor_copy(cq_col.rearrange("p a b -> p (a b)"), ps[:, 4, 0:16]).then_inc(cq_copied, 1)
            dve.wait_ge(cq_copied, 1)
            dve.wait_ge(in_causal, 16)
            attention(16, 8, H_SPLIT["att"], 0, 144, 272, sm_a, mask_a, False)
            plain("att_o", LN["att"], TOK)
            layer_norm(LN["att"], TOK, "ln8")
            ffn(5)
            layer_norm(LN["ffn5"], TOK, None)

        @block.tensor
        def _(pe):
            def three(dst, wh, wl, xh, xl, first, last):
                nc.tensor.matmul(dst, wh, xh, start=first, stop=False, skip_group_check=True)
                nc.tensor.matmul(dst, wh, xl, start=False, stop=False, skip_group_check=True)
                return nc.tensor.matmul(dst, wl, xh, start=False, stop=last, skip_group_check=True)

            def tile(slot, t):
                return w_hi[:, slot, t * P:(t + 1) * P], w_lo[:, slot, t * P:(t + 1) * P]

            def whole(cw, src_hi, src_lo):
                def body(u, slot, i, j, r):
                    pe.wait_ge(w_lo_ready, u + 1)
                    for k in range(KD):
                        ins = three(ps[:, slot, 0:cw.stop - cw.start], *tile(slot, k), src_hi[:, k, cw], src_lo[:, k, cw],
                                    k == 0, k == KD - 1)
                    ins.then_inc(unit_done, 1)
                return body

            def stats(k, cw, pooled):
                n_cols = cw.stop - cw.start
                pe.wait_ge(sums_ready, 2 * k + 2)
                for bank, acc, src, ready in ((6, acc1, y, y_ready), (7, acc2, sq, sq_ready)):
                    nc.tensor.matmul(ps[:, bank, 0:n_cols], ones[:, :], acc[:, cw], start=True, stop=False, skip_group_check=True)
                for n in range(pooled, KD):
                    for bank, src, ready in ((6, y, y_ready), (7, sq, sq_ready)):
                        pe.wait_ge(ready, KD * k + n + 1)
                        ins = nc.tensor.matmul(ps[:, bank, 0:n_cols], ones[:, :], src[:, n, cw], start=False,
                                               stop=n == KD - 1, skip_group_check=True)
                ins.then_inc(stats_ready, 1)

            def ffn(f, src_hi, src_lo, x_count):
                cw = ffn_cols(f)
                n_cols = cw.stop - cw.start
                base = H_SPLIT[f"ffn{f}"]
                pe.wait_ge(x_split, x_count)
                each_unit(pe, f"up{f}", whole(cw, src_hi, src_lo))
                for half in range(2):
                    def down(u, slot, i, j, r):
                        pe.wait_ge(w_lo_ready, u + 1)
                        if half == 0:
                            pe.wait_ge(h_split, base + 2 * i + 2)
                        for kk in range(2):
                            k = bass.ds(2 * i + kk, 1)
                            for q in range(4):
                                dst = ps[:, 4 * (1 - half) + q:4 * (1 - half) + q + 1, 0:n_cols]
                                ins = three(dst, *tile(slot, 4 * kk + q), h_hi[:, k, cw], h_lo[:, k, cw], False, False)
                        ins.then_inc(unit_done, 1)

                    def down_first(u, slot, i):
                        pe.wait_ge(w_lo_ready, u + 1)
                        pe.wait_ge(h_split, base + (2 if half == 0 else NF))
                        for kk in range(2):
                            for q in range(4):
                                ins = three(ps[:, 4 * (1 - half) + q, 0:n_cols], *tile(slot, 4 * kk + q),
                                            h_hi[:, kk, cw], h_lo[:, kk, cw], kk == 0, False)
                        ins.then_inc(unit_done, 1)

                    u = BASE[f"down{f}"] + 11 * half
                    down_first(u, u % RING, 0)
                    each_unit(pe, f"down{f}", lambda u, s, i, j, r: down(u, s, i + 1, j, r), 10, 11 * half + 1)
                stats(LN[f"ffn{f}"], cw, 4)

            def embedding(l, x_count):
                pe.wait_ge(p_split, 2 * (l + 1))
                for i in range(2):
                    u = BASE[f"proj{l}"] + i
                    slot = u % RING
                    pe.wait_ge(w_lo_ready, u + 1)
                    for q in range(4):
                        bank = slot if q < 2 else 4 + i
                        dst = ps[:, bank, (q % 2) * SEQ:(q % 2 + 1) * SEQ]
                        for k in range(2):
                            ins = three(dst, *tile(slot, 2 * q + k), h_hi[:, k, TOK], h_lo[:, k, TOK], k == 0, k == 1)
                    ins.then_inc(unit_done, 1)
                pe.wait_ge(x_split, x_count)
                each_unit(pe, f"gate{l}", whole(TOK, a_hi, a_lo))

            def wide(phase, cw, k, h_count):
                pe.wait_ge(h_split, h_count)
                each_unit(pe, phase, whole(cw, h_hi, h_lo))
                stats(k, cw, 6)

            def attention(first, n_heads, h_base, scores_of, pt, ptm, p_of, value, w0, per):
                for t in range(-1, n_heads):
                    if t >= 0:
                        a = first + t
                        pe.wait_ge(probs, a + 1)
                        if t > 0:
                            pe.wait_ge(turned_sb, per(t - 1))
                            pe.wait_ge(h_split, h_base + t)
                        p0, p1 = p_of(a)
                        k0 = META if ptm is not None else 0
                        for s, src in enumerate((p0[:, k0:k0 + P], p1[:, k0:k0 + P], p1[:, k0 + P:k0 + 2 * P])):
                            ins = nc.tensor.transpose(ps[:, 6, s * P:(s + 1) * P], src, ident)
                        if ptm is not None:
                            for b, p in enumerate((p0, p1)):
                                ins = nc.tensor.matmul(ps[0:META, 7, 256 + b * P:256 + (b + 1) * P], p[:, 0:META], ident,
                                                       start=True, stop=True, skip_group_check=True)
                        ins.then_inc(turned, 1)
                    for nxt in ((0, 1) if t < 0 else (t + 2,)):
                        if nxt < n_heads:
                            a = first + nxt
                            if nxt >= 2:
                                pe.wait_ge(maxed, a - 1)
                            scores_of(nxt, 4 + a % 2).then_inc(scores, 1)
                    if t >= 0:
                        a = first + t
                        pe.wait_ge(turned_sb, per(t))
                        v0, v1, v_meta = value(t)
                        nc.tensor.matmul(ps[:, 7, 0:SEQ], v0, pt[:, 0:SEQ], start=True, stop=False, skip_group_check=True)
                        ins = nc.tensor.matmul(ps[:, 7, P:SEQ], v1, pt[:, SEQ:384], start=False, stop=ptm is None,
                                               skip_group_check=True)
                        if ptm is not None:
                            ins = nc.tensor.matmul(ps[:, 7, 0:SEQ], v_meta, ptm[0:META, :], start=False, stop=True,
                                                   skip_group_check=True)
                        ins.then_inc(mixed, 1)

            pe.wait_ge(x_split, 8)
            each_unit(pe, "mla_in", whole(TOK, a_hi, a_lo))
            pe.wait_ge(zeroed, 1)
            for n in range(6):
                at = 0 if n < 4 else SEQ
                pe.wait_ge(c_copied, 2 * n + 2)
                ins = nc.tensor.matmul(ps[:, 6, at:at + SEQ], ones[:, :], c_sq[:, n, :], start=n in (0, 4), stop=n in (3, 5),
                                       skip_group_check=True)
            ins.then_inc(c_sums, 1)
            pe.wait_ge(c_copied, 13)
            pe.wait_ge(in_con, 16)
            nc.tensor.matmul(ps[:, 7, 0:SEQ], swap, kr_raw, start=True, stop=True).then_inc(kr_swapped, 1)
            for half in range(2):
                pe.wait_ge(c_split, 6)
                for i in range(4):
                    u = BASE[f"mla_qn{half}"] + i
                    pe.wait_ge(w_lo_ready, u + 1)
                    for q in range(2):
                        for k in range(4):
                            ins = three(ps[:, u % RING, q * SEQ:(q + 1) * SEQ], *tile(u % RING, 4 * q + k),
                                        b_hi[:, k, TOK], b_lo[:, k, TOK], k == 0, k == 3)
                    ins.then_inc(unit_done, 1)
                for i in range(3):
                    if i < 2:
                        u = BASE[f"mla_qr{half}"] + i
                        pe.wait_ge(w_lo_ready, u + 1)
                        for q in range(2):
                            for k in range(4):
                                ins = three(ps[:, u % RING, q * SEQ:(q + 1) * SEQ], *tile(u % RING, 4 * q + k),
                                            b_hi[:, k, TOK], b_lo[:, k, TOK], k == 0, k == 3)
                        ins.then_inc(unit_done, 1)
                    if i > 0:
                        pe.wait_ge(qr_copied, 2 * half + i)
                        nc.tensor.matmul(ps[:, 3 + i, :], swap, qr_raw[:, 2 * i - 2:2 * i, :].rearrange("p a b -> p (a b)"),
                                         start=True, stop=True).then_inc(qr_swapped, 1)
                pe.wait_ge(kr_ready, 2)
                for i in range(2):
                    u = BASE[f"mla_kn{half}"] + i
                    pe.wait_ge(w_lo_ready, u + 1)
                    for q in range(4):
                        bank = u % RING if q < 2 else 6 + i
                        for k in range(2):
                            ins = three(ps[:, bank, (q % 2) * SEQ:(q % 2 + 1) * SEQ], *tile(u % RING, 2 * q + k),
                                        b_hi[:, 4 + k, TOK], b_lo[:, 4 + k, TOK], k == 0, k == 1)
                    ins.then_inc(unit_done, 1)
                pe.wait_ge(qr_ready, 4 * half + 4)
                for i in range(2):
                    u = BASE[f"mla_v{half}"] + i
                    pe.wait_ge(w_lo_ready, u + 1)
                    for m in range(2):
                        tokens = slice(META + m * P, META + (m + 1) * P)
                        for k in range(2):
                            w = slice(512 * k, 512 * k + 512)
                            ins = three(ps[:, u % RING if m == 0 else 4 + i, :], b_hi[:, 4 + k, tokens], b_lo[:, 4 + k, tokens],
                                        w_hi[:, u % RING, w], w_lo[:, u % RING, w], k == 0, k == 1)
                    ins.then_inc(unit_done, 1)
                pe.wait_ge(q_copied, 4 * half + 4)
                pe.wait_ge(k_copied, 4 * half + 4)
                pe.wait_ge(v_copied, 4 * half + 4)

                def mla_scores(t, bank):
                    for b, at, width in ((0, 0, P), (1, P, SEQ)):
                        block_q = slice(b * P, (b + 1) * P)
                        dst = ps[:, bank, at:at + width]
                        nc.tensor.matmul(dst, qn[:, t, block_q], kn[:, t, 0:width], start=True, stop=False,
                                         skip_group_check=True)
                        ins = nc.tensor.matmul(dst, qr[:, t // 2, block_q], krm[:, t % 2, 0:width], start=False, stop=True,
                                               skip_group_check=True)
                    return ins

                attention(8 * half, 8, H_SPLIT["mla"] + 8 * half, mla_scores, pt_m, None,
                          lambda a: (sm_m[:, a % 2, 0:P], sm_m[:, a % 2, P:384]),
                          lambda t: (vm[:, 0, t * P:(t + 1) * P], vm[:, 1, t * P:(t + 1) * P], None), 128,
                          lambda t, half=half: 8 * half + t + 1)
            pe.wait_ge(h_split, H_SPLIT["ffn0"])

            def mla_o(u, slot, i, j, r):
                second = r % 2
                pe.wait_ge(w_lo_ready, u + 1)
                for k in range(8):
                    ins = three(ps[:, (slot - second) % RING, 0:SEQ], *tile(slot, k), h_hi[:, 8 * second + k, TOK],
                                h_lo[:, 8 * second + k, TOK], second == 0 and k == 0, second == 1 and k == 7)
                ins.then_inc(unit_done, 1)

            each_unit(pe, "mla_o", mla_o)
            stats(LN["mla"], TOK, 6)
            ffn(0, a_hi, a_lo, X_SPLIT["ln1"])
            embedding(0, X_SPLIT["ple0"])

            pe.wait_ge(x_split, X_SPLIT["ln2"])
            whole(TOK, b_hi, b_lo)(BASE["gla_a"], BASE["gla_a"] % RING, 0, 0, 0)

            def by_token(phase, i, first_bank):
                u = BASE[phase] + i
                slot = u % RING
                pe.wait_ge(w_lo_ready, u + 1)
                for kk in range(2):
                    k = 2 * (i % 4) + kk
                    for m in range(2):
                        tokens = slice(META + m * P, META + (m + 1) * P)
                        w = slice(512 * kk, 512 * kk + 512)
                        ins = three(ps[:, first_bank + m, :], b_hi[:, k, tokens], b_lo[:, k, tokens],
                                    w_hi[:, slot, w], w_lo[:, slot, w], k == 0, k == KD - 1)
                ins.then_inc(unit_done, 1)

            pe.wait_ge(aT_ready, 1)
            for i in range(4):
                by_token("gla_k", i, 0)
            pe.wait_ge(in_wa2, 16)
            for m in range(2):
                ins = nc.tensor.matmul(ps[:, 6 + m, :], g_aT[0:32, m * P:(m + 1) * P], g_wa2[0:32, :], start=True, stop=True)
            ins.then_inc(z_ready, 1)
            for i in range(4):
                by_token("gla_v", i, 2)
            pe.wait_ge(la_ready, 2)
            for m in range(2):
                ins = nc.tensor.matmul(ps[:, 6 + m, :], suffix, g_la[:, m, :], start=True, stop=True)
            ins.then_inc(suf_ready, 1)
            for m in range(2):
                for hd in range(4):
                    ins = nc.tensor.matmul(ps[:, 4, hd * 4 + 2 * m:hd * 4 + 2 * m + 2], g_la[:, m, hd * P:(hd + 1) * P],
                                           chunk_of, start=True, stop=True, skip_group_check=True)
            ins.then_inc(tot_ready, 1)
            pe.wait_ge(gk_copied, 2)
            for i in range(4, 8):
                by_token("gla_v", i, 0)
            pe.wait_ge(gv_copied, 4)
            each_unit(pe, "gla_q", whole(TOK, b_hi, b_lo))
            pe.wait_ge(kdec_ready, 1)
            pe.wait_ge(dec_ready, 1)
            pe.wait_ge(gq_copied, 4)
            for n in range(8):
                u = BASE["gla_r"] + n
                whole(TOK, b_hi, b_lo)(u, u % RING, n, n // 2, n % RING)
                c = n // 2
                m, rows = c // 2, slice(CHUNK * (c % 2), CHUNK * (c % 2 + 1))
                if n % 2 == 0:
                    if c > 0:
                        pe.wait_ge(state_ready, c)
                    for hd in range(4):
                        ins = nc.tensor.matmul(ps[:, 4 + hd // 2, (hd % 2) * 256:(hd % 2 + 1) * 256],
                                               g_k[rows, m, hd * P:(hd + 1) * P], g_v[rows, m, hd * 256:(hd + 1) * 256],
                                               start=True, stop=True, skip_group_check=True)
                    ins.then_inc(upd_ready, 1)
                else:
                    pe.wait_ge(state_ready, c + 1)
                    if c >= 2:
                        pe.wait_ge(go_copied, c - 1)
                    for t in range(8):
                        ins = nc.tensor.matmul(ps[:, 6 + c % 2, t * CHUNK:(t + 1) * CHUNK],
                                               g_S[:, t // 2, (t % 2) * P:(t % 2 + 1) * P],
                                               g_q[:, t // 2, CHUNK * c:CHUNK * (c + 1)], start=True, stop=True,
                                               skip_group_check=True)
                    ins.then_inc(go_ready, 1)
            pe.wait_ge(go_copied, 4)
            pe.wait_ge(go_sq, 1)
            for bank, src in ((4, g_o), (6, g_osq)):
                for hd in range(4):
                    for v in range(2):
                        ins = nc.tensor.matmul(ps[:, bank + hd // 2, (hd % 2) * 256:(hd % 2 + 1) * 256], ones[:, :],
                                               src[:, 2 * hd + v, :], start=v == 0, stop=v == 1, skip_group_check=True)
            ins.then_inc(go_sums, 1)
            wide("gla_o", TOK, LN["gla"], H_SPLIT["ffn1"])
            ffn(1, a_hi, a_lo, X_SPLIT["ln3"])
            embedding(1, X_SPLIT["ple1"])

            pe.wait_ge(meta_lo, 1)
            ffn(2, b_hi, b_lo, X_SPLIT["ln4"])
            pe.wait_ge(x_split, X_SPLIT["ln5"])
            each_unit(pe, "conv_in", whole(slice(0, T), a_hi, a_lo))
            wide("conv_out", slice(0, T), LN["conv"], H_SPLIT["ffn3"])
            ffn(3, a_hi, a_lo, X_SPLIT["ln6"])
            pe.wait_ge(x_split, X_SPLIT["ln7"])
            each_unit(pe, "kv_k", whole(slice(0, T), a_hi, a_lo))

            def turn_values(n):
                pe.wait_ge(vT_copied, n + 1)
                if n >= 2:
                    pe.wait_ge(vs_copied, 2 * (n - 1))
                for at, first, rows in ((0, 0, META), (P, META, P), (2 * P, META + P, P)):
                    ins = nc.tensor.matmul(ps[0:rows, 4 + n % 2, at:at + P], vT[:, n % 2, first:first + rows], ident,
                                           start=True, stop=True, skip_group_check=True)
                ins.then_inc(vt_turned, 1)

            for n in range(8):
                u = BASE["kv_v"] + n
                whole(slice(0, T), a_hi, a_lo)(u, u % RING, n, n // 2, n % RING)
                if n > 0:
                    turn_values(n - 1)
            u = BASE["kv_f"]
            whole(slice(0, T), a_hi, a_lo)(u, u % RING, 0, 0, 0)
            turn_values(7)
            pe.wait_ge(vs_copied, 16)
            ffn(4, a_hi, a_lo, X_SPLIT["ln7"])
            pe.wait_ge(x_split, X_SPLIT["ln8"])
            each_unit(pe, "att_q", whole(TOK, a_hi, a_lo))
            pe.wait_ge(c_ready, 1)
            for b in range(2):
                ins = nc.tensor.matmul(ps[:, 4, 8 * b:8 * b + 8], cum_c[0:8, META + b * P:META + (b + 1) * P], ident[0:8, 0:8],
                                       start=True, stop=True, skip_group_check=True)
            ins.then_inc(cq_ready, 1)
            pe.wait_ge(aq_copied, 8)
            pe.wait_ge(cq_copied, 1)

            def att_scores(t, bank):
                for b, at, width in ((0, 0, META + P), (1, META + P, T)):
                    dst = ps[:, bank, at:at + width]
                    nc.tensor.matmul(dst, a_q[:, t, b * P:(b + 1) * P], k_sh[:, t, 0:width], start=True, stop=False,
                                     skip_group_check=True)
                    ins = nc.tensor.matmul(dst, ident[0:8, t:t + 1].to_broadcast([8, P]), neg_c[0:8, 0:width],
                                           start=False, stop=True, skip_group_check=True)
                return ins

            attention(16, 8, H_SPLIT["att"], att_scores, pt_a, ptm_a,
                      lambda a: (sm_a[:, a % 2, 0:144], sm_a[:, a % 2, 144:416]),
                      lambda t: (v_sh[:, 1, t * P:(t + 1) * P], v_sh[:, 2, t * P:(t + 1) * P],
                                 v_sh[0:META, 0, t * P:(t + 1) * P]), 144,
                      lambda t: 16 + 2 * (t + 1))
            wide("att_o", TOK, LN["att"], H_SPLIT["ffn5"])
            ffn(5, a_hi, a_lo, 96)


def _tiles(w):
    k, n = w.shape
    return w.reshape(k // P, P, n // P, P).transpose(2, 0, 1, 3)


def _units(tiles):
    return tiles.reshape(-1, 8, P, P).transpose(0, 2, 1, 3).reshape(-1, P, UNIT)


def _by_input(w):
    k, n = w.shape
    return w.reshape(k // 256, 2, P, n // 512, 512).transpose(3, 0, 2, 1, 4).reshape(-1, P, UNIT)


def _wider(w, n):
    return np.concatenate([w, np.zeros((w.shape[0], n - w.shape[1]), w.dtype)], axis=1)


def _mla_units(i):
    w = i["mla_w_in"][0]
    yield _units(_tiles(np.concatenate([w, w[:, 768:832]], axis=1)))
    uq = i["mla_w_uq"][0].reshape(512, 16, 192)
    uk = i["mla_w_uk"][0]
    uv = i["mla_w_uv"][0]
    for half in (slice(0, 8), slice(8, 16)):
        wide = slice(half.start * P, half.stop * P)
        yield _units(_tiles(uq[:, half, :P].reshape(512, 1024)))
        yield _units(_tiles(uq[:, half, P:].reshape(512, 512)))
        yield _units(_tiles(uk[:, wide]))
        yield _by_input(uv[:, wide])
    yield _units(_tiles(i["mla_w_o"][0]))


def _ffn_units(gate, up, down):
    g, u = _tiles(gate), _tiles(up)
    yield _units(np.stack([g, u], axis=1))
    d = _tiles(down).reshape(2, 4, NF, P, P).transpose(0, 2, 1, 3, 4)
    yield _units(d)


def _stream(i):
    yield from _mla_units(i)
    for l in range(2):
        up = i["ffn_w_up"][l]
        yield from _ffn_units(up[:, FF:], up[:, :FF], i["ffn_w_down"][l])
        yield _units(_tiles(i["ple_w_proj"][l]))
        yield _units(_tiles(i["ple_w_gate"][l]))
        if l == 0:
            w = i["gla_w_in"][0]
            yield _units(_tiles(_wider(w[:, 3072:3088], P)))
            yield _by_input(w[:, 512:1024])
            yield _by_input(w[:, 1024:2048])
            yield _units(_tiles(w[:, 0:512]))
            yield _units(_tiles(w[:, 2048:3072]))
            yield _units(_tiles(i["gla_w_o"][0]))
    f1 = [(i["ffn1_wg_2"][l], i["ffn1_wu_2"][l], i["ffn1_wd_2"][l]) for l in range(2)]
    f2 = [(i["ffn2_wg_2"][l], i["ffn2_wu_2"][l], i["ffn2_wd_2"][l]) for l in range(2)]
    yield from _ffn_units(*f1[0])
    w = _tiles(i["conv_w_in_2"][0])
    yield _units(np.stack([w[8:16], w[16:24], w[0:8]], axis=1))
    yield _units(_tiles(i["conv_w_out_2"][0]))
    yield from _ffn_units(*f2[0])
    w = i["kv_w_2"]
    yield _units(_tiles(w[:, 0:1024]))
    yield _units(_tiles(w[:, 1024:2048]))
    yield _units(_tiles(_wider(w[:, 2048:2056], P)))
    yield from _ffn_units(*f1[1])
    yield _units(_tiles(i["attn_w_q_2"][0]))
    yield _units(_tiles(i["attn_w_o_2"][0]))
    yield from _ffn_units(*f2[1])


def _cols(v):
    return v.reshape(-1, P).T


def _params(i):
    g2, b2 = i["ln_gain_2"], i["ln_bias_2"]
    gains = [i["ln1_g"][0], i["ln2_g"][0], i["ln1_g"][1], i["ln2_g"][1], *g2[0], *g2[1]]
    biases = [i["ln1_b"][0], i["ln2_b"][0], i["ln1_b"][1], i["ln2_b"][1], *b2[0], *b2[1]]

    def gate_up(v):
        return v.reshape(2, NF, P)[::-1].transpose(1, 0, 2).reshape(2 * NF, P).T

    parts = [_cols(i["mla_q_norm"][0]), _cols(i["mla_kv_norm"][0]), _cols(i["gla_o_norm"][0])]
    parts += [_cols(g) for g in gains] + [_cols(b) for b in biases]
    parts += [gate_up(i["ffn_conv_w"][l, t]) for l in range(2) for t in range(3)]
    parts += [gate_up(i["ffn_conv_b"][l]) for l in range(2)]
    parts += [_cols(i["ple_b_gate"][l]) for l in range(2)]
    parts += [_cols(i["conv_w_2"][0, t]) for t in range(3)]
    fb = np.zeros((P, 1), np.float32)
    fb[0:8, 0] = i["f_bias_2"]
    return np.ascontiguousarray(np.concatenate(parts + [fb], axis=1))


def _constants():
    c = np.zeros((P, NCON), np.float32)
    r = np.arange(P)
    c[:, CCOL["ident"]:CCOL["ident"] + P] = np.eye(P)
    same = r[:, None] // CHUNK == r[None, :] // CHUNK
    c[:, CCOL["suffix"]:CCOL["suffix"] + P] = same & (r[:, None] > r[None, :])
    c[:, CCOL["swap"]:CCOL["swap"] + P] = (r[:, None] ^ 32) == r[None, :]
    c[:, CCOL["chunk_of"]] = r < CHUNK
    c[:, CCOL["chunk_of"] + 1] = r >= CHUNK
    inv = (np.float32(1.0) / np.power(np.float32(10000.0), np.arange(0, 64, 2, dtype=np.float32) / np.float32(64))).astype(np.float32)
    c[:, CCOL["inv_freq"]] = inv[r % 32]
    c[:, CCOL["rope_sign"]] = np.where(r % 64 < 32, -1.0, 1.0)
    c[16, CCOL["one16"]] = 1.0
    q = r[:, None]
    first = np.where(np.arange(META + P)[None, :] <= META + q, 0.0, NEG)
    second = np.where(np.arange(T)[None, :] <= META + P + q, 0.0, NEG)
    return c, np.concatenate([first, second], axis=1).astype(np.float32)


def kernel(**inputs):
    import concourse.bacc as bacc
    from concourse.bass_utils import run_bass_kernel_spmd as run

    i = {name: np.asarray(a) for name, a in inputs.items()}
    consts, causal = _constants()
    wa2 = np.zeros((32, 512), np.float32)
    wa2[0:16] = i["gla_w_a2"][0]
    wa2[16] = i["gla_b_a"][0]
    arrays = {
        "stream": np.concatenate(list(_stream(i)), axis=0),
        "xT": i["x"][0].T,
        "metaT": i["meta_2"].T,
        "pT": i["p"][:, 0].transpose(0, 2, 1),
        "pos": i["positions"],
        "params": _params(i),
        "consts": consts,
        "causal": causal,
        "wa2": wa2,
    }
    nc = bacc.Bacc("TRN2", target_bir_lowering=False, num_devices=1)
    arrays = {name: np.ascontiguousarray(a) for name, a in arrays.items()}
    args = [nc.dram_tensor(name, a.shape, mybir.dt.from_np(a.dtype), kind="ExternalInput").ap() for name, a in arrays.items()]
    out = nc.dram_tensor("out", (D, SEQ), F32, kind="ExternalOutput").ap()
    build(nc, *args, out)
    r = run(nc, [arrays], core_ids=[0])
    return np.ascontiguousarray(r.results[0]["out"].T)[None]
```
